# Optimizing a Trainium2 kernel written in Bass

```python
import math
import jax, jax.numpy as jnp
from jax import lax
import numpy as np

D_MODEL = 1024
BATCH = 1
SEQ = 1024
DEPTH = 1
DEC_BATCH = 8
DEC_SEQ = 4
PAST_LEN = 8192
PAGE_SIZE = 128

N_META = 16
CHUNK = 64
EPS = 1e-6
SSM_EXPAND = 2
D_INNER = SSM_EXPAND * D_MODEL
SSM_HEAD_DIM = 64
SSM_HEADS = D_INNER // SSM_HEAD_DIM
SSM_GROUPS = 4
SSM_STATE = 128
SSM_CONV = 4
SSM_XBC = D_INNER + 2 * SSM_GROUPS * SSM_STATE
GDN_HEADS = 8
GDN_DK = 128
GDN_DV = 128
GDN_CONV = 4
GDN_QKV = GDN_HEADS * (2 * GDN_DK + GDN_DV)
D_FF = 2816
FFN_CONV = 3
IN_SIZES = (D_INNER, SSM_XBC, SSM_HEADS, GDN_QKV, GDN_HEADS, GDN_HEADS, GDN_HEADS * GDN_DV, D_MODEL, D_MODEL)
IN_DIM = sum(IN_SIZES)

kernel_name = "hybrid_ssd_gdn_convffn_meta_step"

def split_cols(t, sizes):
    out = []
    off = 0
    for s in sizes:
        out.append(t[..., off:off + s])
        off += s
    return out

def rmsnorm(x, w):
    xf = x.astype(jnp.float32)
    y = xf * lax.rsqrt(jnp.mean(xf * xf, axis=-1, keepdims=True) + EPS)
    return (y * w.astype(jnp.float32)).astype(x.dtype)

def l2norm(x):
    return x * lax.rsqrt(jnp.sum(x * x, axis=-1, keepdims=True) + EPS)

def causal_dwconv(x, buf, w):
    width = w.shape[0]
    L = x.shape[1]
    xp = jnp.concatenate([buf.astype(x.dtype), x], axis=1)
    y = xp[:, 0:L] * w[0]
    for j in range(1, width):
        y = y + xp[:, j:j + L] * w[j]
    return y, xp[:, L:]

def ssd_segment(x, Bm, Cm, dt, A, h0):
    b, L = x.shape[:2]
    c = math.gcd(L, CHUNK)
    nc = L // c
    hg = SSM_HEADS // SSM_GROUPS

    def to_chunks(t):
        return jnp.moveaxis(t.reshape((b, nc, c) + t.shape[2:]), 1, 0)

    xs = to_chunks(x.reshape(b, L, SSM_GROUPS, hg, SSM_HEAD_DIM))
    dts = to_chunks(dt.reshape(b, L, SSM_GROUPS, hg))
    Bs = to_chunks(Bm)
    Cs = to_chunks(Cm)
    Ag = A.reshape(SSM_GROUPS, hg)
    causal = jnp.tril(jnp.ones((c, c), dtype=bool))

    def step(h, inp):
        xc, Bc, Cc, dtc = inp
        acum = jnp.cumsum(dtc * Ag, axis=1)
        seg = acum[:, :, None] - acum[:, None, :]
        decay = jnp.exp(jnp.where(causal[None, :, :, None, None], seg, -jnp.inf))
        cb = jnp.einsum('bign,bjgn->bijg', Cc, Bc)
        wgt = decay * cb[..., None] * dtc[:, None]
        y = jnp.einsum('bijgh,bjghp->bighp', wgt, xc)
        y = y + jnp.einsum('bign,bghpn->bighp', Cc, h) * jnp.exp(acum)[..., None]
        last = acum[:, -1]
        wj = jnp.exp(last[:, None] - acum) * dtc
        h = h * jnp.exp(last)[..., None, None] + jnp.einsum('bjgh,bjghp,bjgn->bghpn', wj, xc, Bc)
        return h, y

    hG = h0.reshape(b, SSM_GROUPS, hg, SSM_HEAD_DIM, SSM_STATE)
    hG, ys = lax.scan(step, hG, (xs, Bs, Cs, dts))
    y = jnp.moveaxis(ys, 0, 1).reshape(b, L, SSM_HEADS, SSM_HEAD_DIM)
    return y, hG.reshape(b, SSM_HEADS, SSM_HEAD_DIM, SSM_STATE)

def gdn_segment(q, k, v, g, beta, S0):
    b, L = q.shape[:2]
    c = math.gcd(L, CHUNK)
    nc = L // c

    def to_chunks(t):
        t = jnp.moveaxis(t.reshape((b, nc, c) + t.shape[2:]), 1, 0)
        return jnp.moveaxis(t, 3, 2)

    qs, ks, vs, gs, bs = (to_chunks(t) for t in (q, k, v, g, beta))
    incl = jnp.tril(jnp.ones((c, c), dtype=bool))
    strict = jnp.tril(jnp.ones((c, c), dtype=bool), -1)
    eye = jnp.eye(c, dtype=jnp.float32)

    def step(S, inp):
        qc, kc, vc, gc, bc = inp
        gcum = jnp.cumsum(gc, axis=-1)
        seg = gcum[..., :, None] - gcum[..., None, :]
        decay = jnp.exp(jnp.where(incl, seg, -jnp.inf))
        kb = kc * bc[..., None]
        amat = jnp.where(strict, jnp.einsum('bhik,bhjk->bhij', kb, kc) * decay, 0.0)
        rhs = jnp.concatenate([vc * bc[..., None], kb * jnp.exp(gcum)[..., None]], axis=-1)
        sol = lax.linalg.triangular_solve(eye + amat, rhs, left_side=True, lower=True, unit_diagonal=True)
        u, w = sol[..., :GDN_DV], sol[..., GDN_DV:]
        v_new = u - jnp.einsum('bhik,bhkv->bhiv', w, S)
        attn = jnp.einsum('bhik,bhjk->bhij', qc, kc) * decay
        o = jnp.einsum('bhik,bhkv->bhiv', qc * jnp.exp(gcum)[..., None], S) + jnp.einsum('bhij,bhjv->bhiv', attn, v_new)
        last = gcum[..., -1]
        S = S * jnp.exp(last)[..., None, None] + jnp.einsum(
            'bhjk,bhjv->bhkv', kc * jnp.exp(last[..., None] - gcum)[..., None], v_new)
        return S, o

    S, os_ = lax.scan(step, S0, (qs, ks, vs, gs, bs))
    o = jnp.moveaxis(jnp.moveaxis(os_, 3, 2), 0, 1).reshape(b, L, GDN_HEADS, GDN_DV)
    return o, S

def mixer_block(x, s_ssm, s_ssm_conv, s_gdn, s_gdn_conv, segments,
                norm_w, w_in, ssm_conv_w, ssm_conv_b, ssm_dt_bias, ssm_a_log, ssm_d, ssm_norm_w,
                gdn_conv_w, gdn_dt_bias, gdn_a_log, gdn_norm_w, w_ssm_out, w_gdn_out, w_o):
    f32 = jnp.float32
    bsz, L, _ = x.shape
    h = rmsnorm(x, norm_w)
    z, xbc, dt_raw, qkv, a_raw, b_raw, gate, mg_ssm, mg_gdn = split_cols(h @ w_in, IN_SIZES)
    xbc, new_ssm_conv = causal_dwconv(xbc, s_ssm_conv, ssm_conv_w)
    xbc = jax.nn.silu(xbc + ssm_conv_b)
    xs, Bm, Cm = split_cols(xbc, (D_INNER, SSM_GROUPS * SSM_STATE, SSM_GROUPS * SSM_STATE))
    xs = xs.reshape(bsz, L, SSM_HEADS, SSM_HEAD_DIM).astype(f32)
    Bm = Bm.reshape(bsz, L, SSM_GROUPS, SSM_STATE).astype(f32)
    Cm = Cm.reshape(bsz, L, SSM_GROUPS, SSM_STATE).astype(f32)
    dt = jax.nn.softplus((dt_raw + ssm_dt_bias).astype(f32))
    A = -jnp.exp(ssm_a_log.astype(f32))
    qkv, new_gdn_conv = causal_dwconv(qkv, s_gdn_conv, gdn_conv_w)
    qkv = jax.nn.silu(qkv)
    q, k, v = split_cols(qkv, (GDN_HEADS * GDN_DK, GDN_HEADS * GDN_DK, GDN_HEADS * GDN_DV))
    q = l2norm(q.reshape(bsz, L, GDN_HEADS, GDN_DK).astype(f32)) * (GDN_DK ** -0.5)
    k = l2norm(k.reshape(bsz, L, GDN_HEADS, GDN_DK).astype(f32))
    v = v.reshape(bsz, L, GDN_HEADS, GDN_DV).astype(f32)
    g = -jnp.exp(gdn_a_log.astype(f32)) * jax.nn.softplus((a_raw + gdn_dt_bias).astype(f32))
    beta = jax.nn.sigmoid(b_raw.astype(f32))
    hs = s_ssm.astype(f32)
    S = s_gdn.astype(f32)
    y_ssm_parts, y_gdn_parts = [], []
    start = 0
    for n in segments:
        sl = slice(start, start + n)
        y1, hs = ssd_segment(xs[:, sl], Bm[:, sl], Cm[:, sl], dt[:, sl], A, hs)
        y2, S = gdn_segment(q[:, sl], k[:, sl], v[:, sl], g[:, sl], beta[:, sl], S)
        y_ssm_parts.append(y1)
        y_gdn_parts.append(y2)
        start += n
    y_ssm = jnp.concatenate(y_ssm_parts, axis=1) + ssm_d.astype(f32)[:, None] * xs
    y_gdn = jnp.concatenate(y_gdn_parts, axis=1)
    y_ssm = y_ssm.reshape(bsz, L, D_INNER) * jax.nn.silu(z.astype(f32))
    y_ssm = rmsnorm(y_ssm.reshape(bsz, L, SSM_GROUPS, D_INNER // SSM_GROUPS),
                    ssm_norm_w.reshape(SSM_GROUPS, D_INNER // SSM_GROUPS))
    y_ssm = y_ssm.reshape(bsz, L, D_INNER).astype(x.dtype) @ w_ssm_out
    y_gdn = rmsnorm(y_gdn, gdn_norm_w) * jax.nn.silu(gate.reshape(bsz, L, GDN_HEADS, GDN_DV).astype(f32))
    y_gdn = y_gdn.reshape(bsz, L, GDN_HEADS * GDN_DV).astype(x.dtype) @ w_gdn_out
    merged = jax.nn.sigmoid(mg_ssm) * y_ssm + jax.nn.sigmoid(mg_gdn) * y_gdn
    x = x + merged @ w_o
    return x, hs.astype(x.dtype), new_ssm_conv, S.astype(x.dtype), new_gdn_conv

def conv_ffn(x, s_conv, norm_w, w_up, conv_w, conv_b, w_down):
    h = rmsnorm(x, norm_w)
    gt, up = split_cols(h @ w_up, (D_FF, D_FF))
    gt, new_conv = causal_dwconv(gt, s_conv, conv_w)
    return x + (jax.nn.silu(gt + conv_b) * up) @ w_down, new_conv

def run_trunk(x, s_ssm, s_ssm_conv, s_gdn, s_gdn_conv, s_ffn_conv, segments,
              norm_mix_w, w_in, ssm_conv_w, ssm_conv_b, ssm_dt_bias, ssm_a_log, ssm_d, ssm_norm_w,
              gdn_conv_w, gdn_dt_bias, gdn_a_log, gdn_norm_w, w_ssm_out, w_gdn_out, w_o,
              norm_ffn_w, w_up, ffn_conv_w, ffn_conv_b, w_down, norm_f_w):
    o_ssm, o_ssm_conv, o_gdn, o_gdn_conv, o_ffn_conv = [], [], [], [], []
    for l in range(DEPTH):
        x, a1, a2, a3, a4 = mixer_block(
            x, s_ssm[l], s_ssm_conv[l], s_gdn[l], s_gdn_conv[l], segments,
            norm_mix_w[l], w_in[l], ssm_conv_w[l], ssm_conv_b[l], ssm_dt_bias[l], ssm_a_log[l], ssm_d[l],
            ssm_norm_w[l], gdn_conv_w[l], gdn_dt_bias[l], gdn_a_log[l], gdn_norm_w[l],
            w_ssm_out[l], w_gdn_out[l], w_o[l])
        x, a5 = conv_ffn(x, s_ffn_conv[l], norm_ffn_w[l], w_up[l], ffn_conv_w[l], ffn_conv_b[l], w_down[l])
        o_ssm.append(a1); o_ssm_conv.append(a2); o_gdn.append(a3); o_gdn_conv.append(a4); o_ffn_conv.append(a5)
    y = rmsnorm(x, norm_f_w)
    return (y, jnp.stack(o_ssm), jnp.stack(o_ssm_conv), jnp.stack(o_gdn),
            jnp.stack(o_gdn_conv), jnp.stack(o_ffn_conv))

def setup_inputs(seed: int = 0) -> dict:
    key = jax.random.key(seed)
    ks = iter(jax.random.split(key, 48))
    f32 = jnp.float32

    def nrm(shape, scale):
        return scale * jax.random.normal(next(ks), shape, f32)

    def dt_bias(n):
        dt = jnp.exp(jax.random.uniform(next(ks), (DEPTH, n), f32, math.log(1e-3), math.log(1e-1)))
        return dt + jnp.log(-jnp.expm1(-dt))

    def a_log(n):
        return jnp.log(jax.random.uniform(next(ks), (DEPTH, n), f32, 1.0, 16.0))

    return {
        "x_prompt": nrm((BATCH, SEQ, D_MODEL), 1.0),
        "x_sample": nrm((DEC_BATCH, DEC_SEQ, D_MODEL), 1.0),
        "state_ssm": nrm((DEPTH, DEC_BATCH, SSM_HEADS, SSM_HEAD_DIM, SSM_STATE), 0.1),
        "state_ssm_conv": nrm((DEPTH, DEC_BATCH, SSM_CONV - 1, SSM_XBC), 1.0),
        "state_gdn": nrm((DEPTH, DEC_BATCH, GDN_HEADS, GDN_DK, GDN_DV), 0.1),
        "state_gdn_conv": nrm((DEPTH, DEC_BATCH, GDN_CONV - 1, GDN_QKV), 1.0),
        "state_ffn_conv": nrm((DEPTH, DEC_BATCH, FFN_CONV - 1, D_FF), 1.0),
        "meta_tokens": nrm((N_META, D_MODEL), 1.0),
        "norm_mix_w": 1.0 + nrm((DEPTH, D_MODEL), 0.02),
        "w_in": nrm((DEPTH, D_MODEL, IN_DIM), D_MODEL ** -0.5),
        "ssm_conv_w": nrm((DEPTH, SSM_CONV, SSM_XBC), SSM_CONV ** -0.5),
        "ssm_conv_b": nrm((DEPTH, SSM_XBC), 0.01),
        "ssm_dt_bias": dt_bias(SSM_HEADS),
        "ssm_a_log": a_log(SSM_HEADS),
        "ssm_d": 1.0 + nrm((DEPTH, SSM_HEADS), 0.1),
        "ssm_norm_w": 1.0 + nrm((DEPTH, D_INNER), 0.02),
        "gdn_conv_w": nrm((DEPTH, GDN_CONV, GDN_QKV), GDN_CONV ** -0.5),
        "gdn_dt_bias": dt_bias(GDN_HEADS),
        "gdn_a_log": a_log(GDN_HEADS),
        "gdn_norm_w": 1.0 + nrm((DEPTH, GDN_DV), 0.02),
        "w_ssm_out": nrm((DEPTH, D_INNER, D_MODEL), D_INNER ** -0.5),
        "w_gdn_out": nrm((DEPTH, GDN_HEADS * GDN_DV, D_MODEL), (GDN_HEADS * GDN_DV) ** -0.5),
        "w_o": nrm((DEPTH, D_MODEL, D_MODEL), D_MODEL ** -0.5),
        "norm_ffn_w": 1.0 + nrm((DEPTH, D_MODEL), 0.02),
        "w_up": nrm((DEPTH, D_MODEL, 2 * D_FF), D_MODEL ** -0.5),
        "ffn_conv_w": nrm((DEPTH, FFN_CONV, D_FF), FFN_CONV ** -0.5),
        "ffn_conv_b": nrm((DEPTH, D_FF), 0.01),
        "w_down": nrm((DEPTH, D_FF, D_MODEL), D_FF ** -0.5),
        "norm_f_w": 1.0 + nrm((D_MODEL,), 0.02),
    }

def reference(x_prompt, x_sample, state_ssm, state_ssm_conv, state_gdn, state_gdn_conv, state_ffn_conv,
              meta_tokens, norm_mix_w, w_in, ssm_conv_w, ssm_conv_b, ssm_dt_bias, ssm_a_log, ssm_d, ssm_norm_w,
              gdn_conv_w, gdn_dt_bias, gdn_a_log, gdn_norm_w, w_ssm_out, w_gdn_out, w_o,
              norm_ffn_w, w_up, ffn_conv_w, ffn_conv_b, w_down, norm_f_w):
    weights = (norm_mix_w, w_in, ssm_conv_w, ssm_conv_b, ssm_dt_bias, ssm_a_log, ssm_d, ssm_norm_w,
               gdn_conv_w, gdn_dt_bias, gdn_a_log, gdn_norm_w, w_ssm_out, w_gdn_out, w_o,
               norm_ffn_w, w_up, ffn_conv_w, ffn_conv_b, w_down, norm_f_w)
    bp, sp, _ = x_prompt.shape
    dtp = x_prompt.dtype
    xp = jnp.concatenate([jnp.broadcast_to(meta_tokens.astype(dtp), (bp, N_META, D_MODEL)), x_prompt], axis=1)
    z_ssm = jnp.zeros((DEPTH, bp, SSM_HEADS, SSM_HEAD_DIM, SSM_STATE), dtp)
    z_ssm_conv = jnp.zeros((DEPTH, bp, SSM_CONV - 1, SSM_XBC), dtp)
    z_gdn = jnp.zeros((DEPTH, bp, GDN_HEADS, GDN_DK, GDN_DV), dtp)
    z_gdn_conv = jnp.zeros((DEPTH, bp, GDN_CONV - 1, GDN_QKV), dtp)
    z_ffn_conv = jnp.zeros((DEPTH, bp, FFN_CONV - 1, D_FF), dtp)
    yp, p_ssm, p_ssm_conv, p_gdn, p_gdn_conv, p_ffn_conv = run_trunk(
        xp, z_ssm, z_ssm_conv, z_gdn, z_gdn_conv, z_ffn_conv, (N_META, sp), *weights)
    y_prompt = yp[:, N_META:]
    y_sample, s_ssm, s_ssm_conv, s_gdn, s_gdn_conv, s_ffn_conv = run_trunk(
        x_sample, state_ssm, state_ssm_conv, state_gdn, state_gdn_conv, state_ffn_conv,
        (x_sample.shape[1],), *weights)
    return (y_prompt, y_sample, p_ssm, p_ssm_conv, p_gdn, p_gdn_conv, p_ffn_conv,
            s_ssm, s_ssm_conv, s_gdn, s_gdn_conv, s_ffn_conv)


_drawn_inputs = setup_inputs


def setup_inputs(seed=0):
    import zlib

    import numpy as np

    out = dict(_drawn_inputs(seed))
    spreads = {}
    factors = {'ssm_conv_b': 3.012,
     'ssm_norm_w': 5.341,
     'gdn_norm_w': 8.0,
     'norm_ffn_w': 2.972,
     'ffn_conv_b': 8.0,
     'norm_f_w': 2.726}
    for name, (base, spread) in spreads.items():
        noise = np.random.default_rng([zlib.crc32(name.encode()), seed]).standard_normal(out[name].shape)
        drawn = base * np.exp(spread * noise) if base else spread * noise
        out[name] = __import__('jax').numpy.asarray(drawn.astype(out[name].dtype))
    for name, factor in factors.items():
        out[name] = (out[name] * factor).astype(out[name].dtype)
    return out
```

```python
from contextlib import ExitStack, contextmanager

import numpy as np

import concourse.bass as bass
from concourse import mybir

ALU = mybir.AluOpType
ACT = mybir.ActivationFunctionType
AX = mybir.AxisListType.X
F32 = mybir.dt.float32
F32R = mybir.dt.float32r
BF16 = mybir.dt.bfloat16

P = 128
DM = 1024
KD = DM // P
META, SEQ, NB, NT = 16, 1024, 8, 4
TP = META + SEQ
TS = NB * NT
T = TP + TS
C = 104
NC = TP // C
HS, PS, G = 32, 64, 4
HPG = HS // G
HG = 8
H = HS + HG
DI = HS * PS
XT, GT = 24, 24
ZT, OT = 16, 8
NTILE = XT + GT + ZT + OT + 16
NSCAN = XT + GT + ZT + OT
W4 = 4
FF, FT, W3 = 2816, 22, 3
EPS = 1e-6
NCOL = ((0, 358), (358, 358), (716, 356))
TT = -(-T // P)
LAST = T - (TT - 1) * P
assert NC * C == TP


@contextmanager
def phase(nc):
    with nc.cleanup_on_exit(), ExitStack() as ctx:
        yield ctx


class Event:

    def __init__(self, nc, name, per=1):
        self.sem, self.per = nc.alloc_semaphore(name), per

    def at(self, rnd, k=None):
        return self.per * rnd + (self.per if k is None else k) + 1

    def ahead(self, rnd):
        return self.per * rnd + 1


class Loads:

    def __init__(self, nc, name, places, dmas=1, primed=0):
        self.sems = [nc.alloc_semaphore(f"{name}{i}") for i in range(places)]
        self.dmas, self.primed = dmas, primed

    def prime(self, eng):
        for s in self.sems:
            eng.sem_inc(s, self.primed)

    def at(self, rnd):
        return 16 * self.dmas * (rnd + 1) + self.primed

    def ahead(self, rnd):
        return 16 * self.dmas * rnd + self.primed


def prime(eng, *events):
    for e in events:
        eng.sem_inc(e.sem, 1)


def bcast(ap, n):
    return ap.unsqueeze(2).to_broadcast([ap.shape[0], ap.shape[1], n])


def bmid(ap, n):
    return ap.unsqueeze(1).to_broadcast([ap.shape[0], n, ap.shape[1]])


def allocator(ctx, nc):
    def sb(name, shape, dt=F32):
        return ctx.enter_context(nc.sbuf_tensor(name, shape, dt))

    return sb


def transpose_bank(pe, bank, sources, n, ident):
    for i, s in enumerate(sources):
        ins = pe.transpose(bank[0:s.shape[1], i * n:(i + 1) * n], s, ident[0:n, 0:n])
    return ins


def norm_phase(nc, tag, x, w_in, ones, hi=None, lo=None, out=None, x_in=None, con=None, masks=None):
    with phase(nc) as ctx:
        sb = allocator(ctx, nc)
        CN = NCOL[0][1]
        sq, v = sb(f"{tag}_sq", [P, 2, KD, CN]), sb(f"{tag}_v", [P, 2, KD, CN])
        w, eps, lnv, rstd = (sb(f"{tag}_{n}", s) for n, s in (("w", [P, KD]), ("eps", [P, 1]), ("ln", [P, 3, CN]),
                                                              ("rstd", [P, 3, CN])))
        ps = ctx.enter_context(nc.psum_tensor(f"{tag}_ps", [P, 3, 512], F32))
        if con is not None:
            masks_raw = sb("c_raw", [P, N_MASK])
            made, masks_in = Event(nc, "c_made"), Loads(nc, "c_masks_in", 1)
        w_loaded, x_loaded, stored = Loads(nc, f"{tag}_w_in", 1), Loads(nc, f"{tag}_x_in", 3), Loads(nc, f"{tag}_out", 3)
        names = "eps_set squared folded summed ln_done rstd_done scaled hi_done lo_done"
        eps_set, squared, folded, summed, ln_done, rstd_done, scaled, hi_done, lo_done = (
            Event(nc, f"{tag}_{n}", {"scaled": KD, "folded": 2, "hi_done": 2, "lo_done": 2}.get(n, 1)) for n in names.split())
        block = ctx.enter_context(nc.Block())

        @block.sync
        def _(sp):
            sp.dma_start(w[:, :], w_in).then_inc(w_loaded.sems[0], 16)
            for n, (c0, cn) in enumerate(NCOL):
                if x_in is not None:
                    sp.dma_start(x[:, :, c0:c0 + cn], x_in[:, :, c0:c0 + cn]).then_inc(x_loaded.sems[n], 16)
            if con is not None:
                sp.dma_start(masks_raw[:, :], masks).then_inc(masks_in.sems[0], 16)
            for n, (c0, cn) in enumerate(NCOL):
                if out is not None:
                    sp.wait_ge(scaled.sem, scaled.at(n))
                    sp.dma_start(out[:, :, c0:c0 + cn], v[:, n % 2, :, 0:cn]).then_inc(stored.sems[n], 16)
            if out is not None:
                for n in range(3):
                    sp.wait_ge(stored.sems[n], stored.at(0))

        @block.tensor
        def _(pe):
            prime(pe, summed)
            if con is not None:
                pe.wait_ge(made.sem, made.at(0))
            for n, (c0, cn) in enumerate(NCOL):
                pe.wait_ge(folded.sem, folded.at(n))
                for k in range(KD // 4):
                    ins = pe.matmul(ps[:, n, 0:cn], ones[:, :], sq[:, n % 2, k, 0:cn], start=(k == 0), stop=(k == KD // 4 - 1))
                ins.then_inc(summed.sem, 1)

        @block.scalar
        def _(act):
            prime(act, squared, ln_done, rstd_done, hi_done)

            def square(n):
                c0, cn = NCOL[n]
                if x_in is not None:
                    act.wait_ge(x_loaded.sems[n], x_loaded.at(0))
                if n >= 2:
                    act.wait_ge(summed.sem, summed.at(n - 2))
                act.activation(sq[:, n % 2, :, 0:cn], x[:, :, c0:c0 + cn], ACT.Square).then_inc(squared.sem, 1)

            square(0)
            act.wait_ge(eps_set.sem, eps_set.at(0))
            for n, (c0, cn) in enumerate(NCOL):
                if n < 2:
                    square(n + 1)
                act.wait_ge(summed.sem, summed.at(n))
                act.activation(lnv[:, n, 0:cn], ps[:, n, 0:cn], ACT.Ln, bias=eps[:, 0:1], scale=1.0 / DM).then_inc(ln_done.sem, 1)
                act.wait_ge(ln_done.sem, ln_done.at(n))
                act.activation(rstd[:, n, 0:cn], lnv[:, n, 0:cn], ACT.Exp, scale=-0.5).then_inc(rstd_done.sem, 1)
                if hi is not None:
                    for half in range(2):
                        ks = slice(KD // 2 * half, KD // 2 * (half + 1))
                        act.wait_ge(scaled.sem, scaled.at(n, KD // 2 * (half + 1)))
                        act.activation(hi[:, ks, c0:c0 + cn], v[:, n % 2, ks, 0:cn], ACT.Copy).then_inc(hi_done.sem, 1)

        @block.vector
        def _(dve):
            prime(dve, eps_set, folded, scaled, lo_done)
            dve.memset(eps[:, :], EPS).then_inc(eps_set.sem, 1)

            def fold(n):
                cn = NCOL[n][1]
                dve.wait_ge(squared.sem, squared.at(n))
                for step, half in enumerate((KD // 2, KD // 4)):
                    if step:
                        dve.wait_ge(folded.sem, folded.at(n, step))
                    dve.tensor_tensor(sq[:, n % 2, 0:half, 0:cn], sq[:, n % 2, 0:half, 0:cn],
                                      sq[:, n % 2, half:2 * half, 0:cn], ALU.add).then_inc(folded.sem, 1)

            fold(0)
            dve.wait_ge(w_loaded.sems[0], w_loaded.at(0))
            for n, (c0, cn) in enumerate(NCOL):
                if n < 2:
                    fold(n + 1)
                dve.wait_ge(rstd_done.sem, rstd_done.at(n))
                if x_in is not None:
                    dve.wait_ge(x_loaded.sems[n], x_loaded.at(0))
                if n >= 2:
                    if hi is not None:
                        dve.wait_ge(lo_done.sem, lo_done.at(n - 2))
                    else:
                        dve.wait_ge(stored.sems[n - 2], stored.at(0))
                for k in range(KD):
                    dve.scalar_tensor_tensor(out=v[:, n % 2, k, 0:cn], in0=x[:, k, c0:c0 + cn],
                                                       scalar=w[:, k:k + 1], in1=rstd[:, n, 0:cn],
                                                       op0=ALU.mult, op1=ALU.mult).then_inc(scaled.sem, 1)
                if hi is not None:
                    for half in range(2):
                        ks = slice(KD // 2 * half, KD // 2 * (half + 1))
                        dve.wait_ge(hi_done.sem, hi_done.at(n, half + 1))
                        dve.wait_ge(scaled.sem, scaled.at(n, KD // 2 * (half + 1)))
                        dve.tensor_tensor(lo[:, ks, c0:c0 + cn], v[:, n % 2, ks, 0:cn],
                                          hi[:, ks, c0:c0 + cn].bitcast(F32), ALU.subtract).then_inc(lo_done.sem, 1)
            if con is not None:
                dve.wait_ge(masks_in.sems[0], masks_in.at(0))
                at = 0
                for name, n, _ in MASKS:
                    dve.tensor_copy(con[name][:, :], masks_raw[:, at:at + n])
                    at += n

        @block.gpsimd
        def _(pool):
            if con is not None:
                prime(pool, made)
                pool.memset(con["ones"][:, :], 1.0).then_inc(made.sem, 1)
                pool.memset(con["selT"][:, :, :], 0.0).then_inc(made.sem, 1)
                for a in range(3):
                    pool.wait_ge(made.sem, made.at(a + 1))
                    pool.affine_select(out=con["selT"][0:3 * H, :, :], in_=con["selT"][0:3 * H, :, :],
                                       compare_op=ALU.not_equal, fill=1.0, base=-a * H,
                                       pattern=[[-1, H], [0, C]], channel_multiplier=1).then_inc(made.sem, 1)


def gates_phase(nc, d, hi, lo, tab, con):
    NCH = NC + 1
    with phase(nc) as ctx:
        sb = allocator(ctx, nc)
        wraw, whi, wlo = sb("gw", [P, KD, 48]), sb("gwh", [P, KD, 48], F32R), sb("gwl", [P, KD, 48], F32R)
        bias, alog, rate = sb("gbias", [P, 48]), sb("galog", [P, H]), sb("grate", [P, H])
        raw, size, soft = sb("graw", [P, NCH, 48]), sb("gsize", [P, NCH, 48]), sb("gsoft", [P, NCH, 48])
        small, logs = sb("gsmall", [P, NCH, 48]), sb("glogs", [P, NCH, 48])
        adt, acc, rest = sb("gadt", [P, NCH, H]), sb("gacc", [P, NCH, H]), sb("grest", [P, 2, NCH, H])
        diff, eb = sb("gdiff", [P, NCH, H]), sb("geb", [P, 2, NCH, HG])
        parts = sb("gparts", [P, NCH, 3, H], BF16)
        by_channel = sb("gby_channel", [48, T])
        ps = ctx.enter_context(nc.psum_tensor("gps", [P, 6, 512], F32))
        psb = ctx.enter_context(nc.psum_tensor("gpsb", [P, 2, 1024], BF16))
        w_in, rows_in = Loads(nc, "gw_in", 1), Loads(nc, "g_rows_in", 1, 2)
        names = """zeroed w_hi w_lo product gathered raw_mm raw_done size_done small_done logs_done soft_done eb_done eb1_done beta_done
                   rate_done adt_done sums_mm acc_done decays_done last_done diff_done weights_done be_done parts_done
                   turned acct_done nacct_done rest_done dt_done decays2_done""".split()
        ev = {n: Event(nc, f"g_{n}") for n in names}
        block = ctx.enter_context(nc.Block())

        @block.sync
        def _(sp):
            sp.dma_start(wraw[:, :, :], d["w_small"]).then_inc(w_in.sems[0], 16)
            sp.dma_start(bias[:, :], d["gate_bias"].to_broadcast([P, 48])).then_inc(rows_in.sems[0], 16)
            sp.dma_start(alog[:, :], d["a_log"].to_broadcast([P, H])).then_inc(rows_in.sems[0], 16)

        @block.tensor
        def _(pe):
            prime(pe, ev["product"], ev["raw_mm"], ev["sums_mm"], ev["turned"])
            pe.wait_ge(ev["w_lo"].sem, ev["w_lo"].at(0, 1))
            for n, (c0, cn) in enumerate(NCOL):
                for k in range(KD):
                    for a, (l, r) in enumerate(((whi, hi), (whi, lo), (wlo, hi))):
                        ins = pe.matmul(ps[0:48, 3 + n, 0:cn], l[:, k, :], r[:, k, c0:c0 + cn],
                                        start=(k == 0 and a == 0), stop=(k == KD - 1 and a == 2))
                ins.then_inc(ev["product"].sem, 1)
            for t in range(NCH):
                n = C if t < NC else TS
                pe.wait_ge(ev["gathered"].sem, ev["gathered"].at(0, min(3, -(-(t * C + n) // NCOL[0][1]))))
                ins = pe.transpose(ps[0:n, t // 6, (t % 6) * 48:(t % 6) * 48 + 48], by_channel[:, t * C:t * C + n],
                                   con["ident"][0:48, 0:48])
            ins.then_inc(ev["raw_mm"].sem, 1)
            pe.wait_ge(ev["adt_done"].sem, ev["adt_done"].at(0, 1))
            pe.matmul(ps[0:C, 2, 0:NC * H], con["tri"][0:C, 0:C],
                      adt[0:C, 0:NC, :].rearrange("p t h -> p (t h)"), start=True, stop=True)
            pe.matmul(ps[0:TS, 2, NC * H:NCH * H], con["tri_s"][0:TS, :], adt[0:TS, NC, :], start=True, stop=True)
            pe.matmul(ps[:, 3, 0:NC * H], con["ones"][0:C, :],
                      adt[0:C, 0:NC, :].rearrange("p t h -> p (t h)"), start=True, stop=True)
            for b in range(NB):
                pe.matmul(ps[:, 4, b * H:(b + 1) * H], con["seq_wide"][0:TS, b, :], adt[0:TS, NC, :],
                          start=True, stop=True)
            pe.matmul(ps[0:TS, 5, 0:H], con["same"][0:TS, :], adt[0:TS, NC, :],
                                      start=True, stop=True).then_inc(ev["sums_mm"].sem, 1)
            pe.wait_ge(ev["parts_done"].sem, ev["parts_done"].at(0, 3))
            for t in range(NCH):
                n = C if t < NC else TS
                ins = pe.transpose(psb[0:3 * H, t // 9, t % 9 * C:t % 9 * C + n],
                                   parts[0:n, t, :, :].rearrange("p a h -> p (a h)"), con["identb"][0:n, 0:n])
            ins.then_inc(ev["turned"].sem, 1)

        @block.scalar
        def _(act):
            prime(act, ev["w_hi"], ev["rate_done"], ev["size_done"], ev["small_done"], ev["eb_done"],
                  ev["logs_done"], ev["decays_done"], ev["decays2_done"], ev["weights_done"], ev["nacct_done"])
            act.wait_ge(w_in.sems[0], w_in.at(0))
            act.activation(whi[:, :, :], wraw[:, :, :], ACT.Copy).then_inc(ev["w_hi"].sem, 1)
            act.wait_ge(rows_in.sems[0], rows_in.at(0))
            act.activation(rate[:, :], alog[:, :], ACT.Exp).then_inc(ev["rate_done"].sem, 1)
            act.wait_ge(ev["raw_done"].sem, ev["raw_done"].at(0, 3))
            act.activation(size[0:C, :, :], raw[0:C, :, :], ACT.Abs).then_inc(ev["size_done"].sem, 1)
            act.wait_ge(ev["size_done"].sem, ev["size_done"].at(0, 1))
            act.activation(small[0:C, :, :], size[0:C, :, :], ACT.Exp, scale=-1.0).then_inc(ev["small_done"].sem, 1)
            act.activation(eb[0:C, 0, :, :], raw[0:C, :, H:48], ACT.Exp, scale=-1.0).then_inc(ev["eb_done"].sem, 1)
            act.wait_ge(ev["small_done"].sem, ev["small_done"].at(0, 1))
            act.activation(logs[0:C, :, :], small[0:C, :, :], ACT.Ln, bias=1.0).then_inc(ev["logs_done"].sem, 1)
            act.wait_ge(ev["acc_done"].sem, ev["acc_done"].at(0, 2))
            act.activation(tab["E"][0:C, :, :], acc[0:C, :, :], ACT.Exp).then_inc(ev["decays_done"].sem, 1)
            act.activation(tab["EL"][:, 0:NC, :].rearrange("p t h -> p (t h)"), ps[:, 3, 0:NC * H], ACT.Exp)
            act.activation(tab["EL"][:, NC:, :].rearrange("p t h -> p (t h)"), ps[:, 4, 0:NB * H], ACT.Exp).then_inc(ev["decays2_done"].sem, 1)
            act.wait_ge(ev["diff_done"].sem, ev["diff_done"].at(0, 1))
            act.wait_ge(ev["last_done"].sem, ev["last_done"].at(0, 1))
            act.activation(tab["W"][0:C, :, :], diff[0:C, :, :], ACT.Exp).then_inc(ev["weights_done"].sem, 1)
            act.wait_ge(ev["turned"].sem, ev["turned"].at(0, 1))
            act.activation(tab["naccT"][0:3 * H, 0:9 * C], psb[0:3 * H, 0, 0:9 * C], ACT.Copy, scale=-1.0)
            act.activation(tab["naccT"][0:3 * H, 9 * C:T], psb[0:3 * H, 1, 0:T - 9 * C],
                                              ACT.Copy, scale=-1.0).then_inc(ev["nacct_done"].sem, 1)

        @block.vector
        def _(dve):
            prime(dve, ev["zeroed"], ev["gathered"], ev["w_lo"], ev["raw_done"], ev["soft_done"], ev["adt_done"], ev["dt_done"],
                  ev["eb1_done"], ev["beta_done"], ev["acc_done"], ev["last_done"], ev["parts_done"],
                  ev["rest_done"], ev["diff_done"], ev["be_done"])
            dve.memset(acc[:, :, :], 0.0)
            dve.memset(diff[:, :, :], 0.0)
            dve.memset(raw[:, :, :], 0.0).then_inc(ev["zeroed"].sem, 1)
            dve.wait_ge(ev["w_hi"].sem, ev["w_hi"].at(0, 1))
            dve.tensor_tensor(wlo[:, :, :], wraw[:, :, :], whi[:, :, :].bitcast(F32), ALU.subtract).then_inc(ev["w_lo"].sem, 1)
            dve.wait_ge(rows_in.sems[0], rows_in.at(0))
            dve.wait_ge(ev["zeroed"].sem, ev["zeroed"].at(0, 1))
            for n, (c0, cn) in enumerate(NCOL):
                dve.wait_ge(ev["product"].sem, ev["product"].at(0, n + 1))
                dve.tensor_copy(by_channel[:, c0:c0 + cn], ps[0:48, 3 + n, 0:cn]).then_inc(ev["gathered"].sem, 1)
            dve.wait_ge(ev["raw_mm"].sem, ev["raw_mm"].at(0, 1))
            dve.tensor_tensor(raw[0:C, 0:6, :], ps[0:C, 0, 0:288].rearrange("p (t h) -> p t h", h=48),
                                               bmid(bias[0:C, :], 6), ALU.add).then_inc(ev["raw_done"].sem, 1)
            dve.tensor_tensor(raw[0:C, 6:NC, :],
                                               ps[0:C, 1, 0:(NC - 6) * 48].rearrange("p (t h) -> p t h", h=48),
                                               bmid(bias[0:C, :], NC - 6), ALU.add).then_inc(ev["raw_done"].sem, 1)
            dve.tensor_tensor(raw[0:TS, NC, :], ps[0:TS, 1, (NC - 6) * 48:(NC - 5) * 48],
                                               bias[0:TS, :], ALU.add).then_inc(ev["raw_done"].sem, 1)
            dve.wait_ge(ev["logs_done"].sem, ev["logs_done"].at(0, 1))
            dve.wait_ge(ev["raw_done"].sem, ev["raw_done"].at(0, 3))
            dve.scalar_tensor_tensor(
                out=soft[0:C, :, :], in0=raw[0:C, :, :], scalar=0.0, in1=logs[0:C, :, :], op0=ALU.max, op1=ALU.add).then_inc(ev["soft_done"].sem, 1)
            dve.wait_ge(ev["soft_done"].sem, ev["soft_done"].at(0, 1))
            dve.wait_ge(ev["rate_done"].sem, ev["rate_done"].at(0, 1))
            dve.scalar_tensor_tensor(
                out=adt[0:C, :, :], in0=soft[0:C, :, 0:H], scalar=-1.0, in1=bmid(rate[0:C, :], NCH),
                op0=ALU.mult, op1=ALU.mult).then_inc(ev["adt_done"].sem, 1)
            dve.tensor_copy(tab["dt"][0:C, :, :], soft[0:C, :, 0:HS]).then_inc(ev["dt_done"].sem, 1)
            dve.wait_ge(ev["eb_done"].sem, ev["eb_done"].at(0, 1))
            dve.tensor_scalar(eb[0:C, 1, :, :], eb[0:C, 0, :, :], 1.0, None, ALU.add).then_inc(ev["eb1_done"].sem, 1)
            dve.wait_ge(ev["eb1_done"].sem, ev["eb1_done"].at(0, 1))
            dve.reciprocal(tab["beta"][0:C, :, :], eb[0:C, 1, :, :]).then_inc(ev["beta_done"].sem, 1)
            dve.wait_ge(ev["sums_mm"].sem, ev["sums_mm"].at(0, 1))
            dve.tensor_copy(acc[0:C, 0:NC, :].rearrange("p t h -> p (t h)"), ps[0:C, 2, 0:NC * H]).then_inc(ev["acc_done"].sem, 1)
            dve.tensor_copy(acc[0:TS, NC, :], ps[0:TS, 2, NC * H:NCH * H]).then_inc(ev["acc_done"].sem, 1)
            dve.wait_ge(ev["acc_done"].sem, ev["acc_done"].at(0, 2))
            dve.wait_ge(ev["decays_done"].sem, ev["decays_done"].at(0, 1))
            dve.tensor_tensor(diff[0:TS, NC, :], ps[0:TS, 5, 0:H], acc[0:TS, NC, :], ALU.subtract).then_inc(ev["last_done"].sem, 1)
            dve.tensor_copy(parts[0:C, :, 0, :], acc[0:C, :, :]).then_inc(ev["parts_done"].sem, 1)
            dve.wait_ge(ev["parts_done"].sem, ev["parts_done"].at(0, 1))
            dve.tensor_tensor(rest[0:C, 0, :, :], acc[0:C, :, :], parts[0:C, :, 0, :], ALU.subtract).then_inc(ev["rest_done"].sem, 1)
            dve.wait_ge(ev["rest_done"].sem, ev["rest_done"].at(0, 1))
            dve.tensor_copy(parts[0:C, :, 1, :], rest[0:C, 0, :, :]).then_inc(ev["parts_done"].sem, 1)
            dve.wait_ge(ev["parts_done"].sem, ev["parts_done"].at(0, 2))
            dve.tensor_tensor(rest[0:C, 1, :, :], rest[0:C, 0, :, :], parts[0:C, :, 1, :],
                                                ALU.subtract).then_inc(ev["rest_done"].sem, 1)
            dve.wait_ge(ev["rest_done"].sem, ev["rest_done"].at(0, 2))
            dve.tensor_copy(parts[0:C, :, 2, :], rest[0:C, 1, :, :]).then_inc(ev["parts_done"].sem, 1)
            dve.wait_ge(ev["decays2_done"].sem, ev["decays2_done"].at(0, 1))
            dve.tensor_tensor(diff[0:C, 0:NC, :].rearrange("p t h -> p (t h)"), ps[0:C, 3, 0:NC * H],
                                                acc[0:C, 0:NC, :].rearrange("p t h -> p (t h)"), ALU.subtract).then_inc(ev["diff_done"].sem, 1)
            dve.wait_ge(ev["beta_done"].sem, ev["beta_done"].at(0, 1))
            dve.scalar_tensor_tensor(out=tab["nBE"][0:C, :, :], in0=tab["beta"][0:C, :, :], scalar=-1.0,
                                     in1=tab["E"][0:C, :, HS:H], op0=ALU.mult, op1=ALU.mult).then_inc(ev["be_done"].sem, 1)
            dve.wait_ge(ev["turned"].sem, ev["turned"].at(0, 1))
            dve.wait_ge(ev["nacct_done"].sem, ev["nacct_done"].at(0, 1))
            dve.tensor_copy(tab["accT"][0:3 * H, 0:9 * C], psb[0:3 * H, 0, 0:9 * C])
            dve.tensor_copy(tab["accT"][0:3 * H, 9 * C:T], psb[0:3 * H, 1, 0:T - 9 * C])


def project_phase(nc, d, hi, lo, scratch):
    CT = XT + GT
    UW, UP = 3 + TP + 7 * NB, TP + 7 * NB
    with phase(nc) as ctx:
        sb = allocator(ctx, nc)
        w = sb("pw", [P, 2, KD, P])
        whi = [sb(f"pwh{u}", [P, KD, P], F32R) for u in range(2)]
        wlo = [sb(f"pwl{u}", [P, KD, P], F32R) for u in range(2)]
        U, Y, O = sb("pU", [P, 2, UW]), sb("pY", [P, 2, 2, UW]), sb("pO", [P, 2, T])
        spare = sb("pspare", [P, 4])
        old, new = sb("pold", [P, CT, NB * 3]), sb("pnew", [P, CT, 27])
        cw, cb = sb("pcw", [P, CT, W4]), sb("pcb", [P, CT])
        ps = ctx.enter_context(nc.psum_tensor("pps", [P, 6, 512], F32))
        w_in = Loads(nc, "pw_in", 2)
        consts_in = Loads(nc, "p_consts_in", 1, 3)
        stored, new_out = Loads(nc, "p_stored", 2, primed=16), Loads(nc, "p_new_out", 1)

        def pair(name, per=1):
            return [Event(nc, f"{name}{u}", per) for u in range(2)]

        hi_done, lo_done, product, evacuated, finished = (pair("w_hi"), pair("w_lo"), pair("product"),
                                                          pair("evacuated", 4), pair("finished", 2))
        tap, old_put, new_got = pair("tap", 4), pair("old_put"), pair("new_got", 2)
        plain = pair("plain", 3)
        zero = Event(nc, "p_zero")
        block = ctx.enter_context(nc.Block())

        def seqs(ap):
            return ap[:, ap.shape[1] - 7 * NB:].rearrange("p (b t) -> p b t", t=7)

        def stages(eng, body, start=lambda kind: None):
            for kind, first, end in (("conv", 0, CT), ("silu", CT, NSCAN), ("sigmoid", NSCAN, NTILE - 2)):
                start(kind)
                with eng.Fori(first // 2, end // 2) as i:
                    for u in range(2):
                        body(2 * i + u, u, i, kind)
            for u in range(2):
                body(NTILE - 2 + u, u, NTILE // 2 - 1, "sigmoid")

        @block.sync
        def _(sp):
            stored.prime(sp)
            for u in range(2):
                sp.dma_start(w[:, u, :, :], d["w_in"][u]).then_inc(w_in.sems[u], 16)
            sp.dma_start(cw[:, :, :], d["conv_w"]).then_inc(consts_in.sems[0], 16)
            sp.dma_start(cb[:, :], d["conv_b"]).then_inc(consts_in.sems[0], 16)
            sp.dma_start(old[:, :, :], d["conv_old"]).then_inc(consts_in.sems[0], 16)

            def store(m, u, i, kind):
                if kind == "conv":
                    sp.wait_ge(finished[u].sem, finished[u].at(i))
                    r = i
                else:
                    sp.wait_ge(plain[u].sem, plain[u].at(i - CT // 2))
                sp.dma_start(scratch[bass.ds(m, 1)].rearrange("a p n -> p a n"), O[:, u:u + 1, :]).then_inc(stored.sems[u], 16)

            def body(m, u, i, kind):
                if not isinstance(m, int):
                    sp.wait_ge(lo_done[u].sem, lo_done[u].at(i))
                    sp.dma_start(w[:, u:u + 1, :, :],
                                         d["w_in"][bass.ds(m + 2, 1)].rearrange("a p k n -> p a k n")).then_inc(w_in.sems[u], 16)
                store(m, u, i, kind)

            stages(sp, body)
            for u in range(2):
                sp.wait_ge(new_got[u].sem, new_got[u].at(CT // 2 - 1))
            sp.dma_start(d["conv_new"], new[:, :, :]).then_inc(new_out.sems[0], 16)
            for u in range(2):
                sp.wait_ge(stored.sems[u], stored.at(NTILE // 2 - 1))
            sp.wait_ge(new_out.sems[0], new_out.at(0))

        @block.tensor
        def _(pe):
            prime(pe, *product)

            def body(m, u, i, kind):
                pe.wait_ge(lo_done[u].sem, lo_done[u].at(i))
                if kind == "conv":
                    pe.wait_ge(evacuated[u].sem, evacuated[u].ahead(i))
                else:
                    pe.wait_ge(evacuated[u].sem, evacuated[u].ahead(CT // 2))
                    pe.wait_ge(plain[u].sem, plain[u].ahead(i - CT // 2))
                for n, (c0, cn) in enumerate(NCOL):
                    for k in range(KD):
                        for a, (l, r) in enumerate(((whi, hi), (whi, lo), (wlo, hi))):
                            ins = pe.matmul(ps[:, 3 * u + n, 0:cn], l[u][:, k, :], r[:, k, c0:c0 + cn],
                                            start=(k == 0 and a == 0), stop=(k == KD - 1 and a == 2))
                ins.then_inc(product[u].sem, 1)

            stages(pe, body)

        @block.scalar
        def _(act):
            prime(act, *hi_done, *evacuated, *finished, *plain)

            def split(m, u, i):
                act.wait_ge(w_in.sems[u], 16 * i + 16)
                act.wait_ge(product[u].sem, product[u].ahead(i))
                act.activation(whi[u][:, :, :], w[:, u, :, :], ACT.Copy).then_inc(hi_done[u].sem, 1)

            def body(m, u, i, kind):
                if not (isinstance(m, int) and m == NTILE - 1):
                    split(m + 1, 1 - u, i + u)
                act.wait_ge(product[u].sem, product[u].at(i))
                if kind == "conv":
                    act.wait_ge(tap[u].sem, tap[u].ahead(i))
                    act.wait_ge(new_got[u].sem, new_got[u].ahead(i))
                    for n, (c0, cn) in enumerate(NCOL):
                        cp = min(cn, TP - c0)
                        act.activation(U[:, u, 3 + c0:3 + c0 + cp], ps[:, 3 * u + n, 0:cp], ACT.Copy).then_inc(evacuated[u].sem, 1)
                    act.activation(
                        seqs(U[:, u, :])[:, :, 3:7], ps[:, 3 * u + 2, TP - 716:TP - 716 + TS].rearrange(
                            "p (b t) -> p b t", t=NT), ACT.Copy).then_inc(evacuated[u].sem, 1)
                    act.wait_ge(tap[u].sem, tap[u].at(i))
                    stored_before(act, u, i)
                    act.activation(O[:, u, 0:TP], Y[:, u, 1, 0:TP], ACT.Silu).then_inc(finished[u].sem, 1)
                    act.activation(O[:, u, TP:T].rearrange("p (b t) -> p b t", t=NT),
                                                  seqs(Y[:, u, 1, :])[:, :, 0:NT], ACT.Silu).then_inc(finished[u].sem, 1)
                else:
                    stored_before(act, u, i)
                    for n, (c0, cn) in enumerate(NCOL):
                        act.activation(O[:, u, c0:c0 + cn], ps[:, 3 * u + n, 0:cn],
                                                   ACT.Silu if kind == "silu" else ACT.Sigmoid).then_inc(plain[u].sem, 1)

            def stored_before(eng, u, i):
                eng.wait_ge(stored.sems[u], stored.ahead(i))

            def table(kind):
                n = {"conv": 1, "silu": 2, "sigmoid": 3}[kind]
                act.activation(spare[:, n:n + 1], spare[:, 0:1], ACT.Sigmoid if kind == "sigmoid" else ACT.Silu)
                if kind == "conv":
                    split(0, 0, 0)

            act.wait_ge(zero.sem, zero.at(0))
            stages(act, body, table)

        @block.vector
        def _(dve):
            prime(dve, zero, *lo_done, *tap)
            for u in range(2):
                dve.memset(U[:, u, 0:3], 0.0)
            ins = dve.memset(spare[:, :], 0.0)
            ins.then_inc(zero.sem, 1)
            dve.wait_ge(consts_in.sems[0], consts_in.at(0))
            dve.wait_ge(zero.sem, zero.at(0))

            def split(m, u, i):
                dve.wait_ge(hi_done[u].sem, hi_done[u].at(i))
                dve.tensor_tensor(wlo[u][:, :, :], w[:, u, :, :], whi[u][:, :, :].bitcast(F32),
                                                ALU.subtract).then_inc(lo_done[u].sem, 1)

            def body(m, u, i, kind):
                if not (isinstance(m, int) and m == NTILE - 1):
                    split(m + 1, 1 - u, i + u)
                if kind != "conv":
                    return
                dve.wait_ge(evacuated[u].sem, evacuated[u].at(i))
                dve.wait_ge(old_put[u].sem, old_put[u].at(i))
                dve.wait_ge(finished[u].sem, finished[u].ahead(i))
                dve.tensor_scalar(Y[:, u, 0, 0:UP], U[:, u, 0:UP], cw[:, bass.ds(m, 1), 0:1],
                                            cb[:, bass.ds(m, 1)], ALU.mult, ALU.add).then_inc(tap[u].sem, 1)
                for j in range(1, W4):
                    dve.wait_ge(tap[u].sem, tap[u].at(i, j))
                    dve.scalar_tensor_tensor(
                        out=Y[:, u, j % 2, 0:UP], in0=U[:, u, j:j + UP], scalar=cw[:, bass.ds(m, 1), j:j + 1],
                        in1=Y[:, u, 1 - j % 2, 0:UP], op0=ALU.mult, op1=ALU.add).then_inc(tap[u].sem, 1)

            split(0, 0, 0)
            stages(dve, body)

        @block.gpsimd
        def _(pool):
            prime(pool, *old_put, *new_got)
            pool.wait_ge(consts_in.sems[0], consts_in.at(0))
            with pool.Fori(0, CT // 2) as i:
                for u in range(2):
                    pool.wait_ge(tap[u].sem, tap[u].ahead(i))
                    pool.tensor_copy(
                        seqs(U[:, u, :])[:, :, 0:3],
                        old[:, bass.ds(2 * i + u, 1), :].rearrange("p a (b t) -> p (a b) t", t=3)).then_inc(old_put[u].sem, 1)
                    pool.wait_ge(evacuated[u].sem, evacuated[u].at(i))
                    pool.tensor_copy(new[:, bass.ds(2 * i + u, 1), 0:3], U[:, u:u + 1, TP:TP + 3]).then_inc(new_got[u].sem, 1)
                    pool.tensor_copy(
                        new[:, bass.ds(2 * i + u, 1), 3:27].rearrange("p a (b t) -> p (a b) t", t=3),
                        seqs(U[:, u, :])[:, :, 4:7]).then_inc(new_got[u].sem, 1)


def scan_phase(nc, d, tab, con, scratch, mixed, running):
    c = TS if running else C
    levels = 2 if running else 7
    lev = con["levels_s" if running else "levels"][:, :].rearrange("p (l i) -> p l i", i=c)
    late = con["late_s" if running else "late"]
    nseq = NB if running else 1
    HPL = 3
    NHB = HG // 2
    XG, ZG = HPG * PS, NHB * P
    tag = "run" if running else "scan"
    with phase(nc) as ctx:
        sb = allocator(ctx, nc)

        def buf(name, shape, dt=F32):
            return sb(f"{tag}_{name}", shape, dt)

        cd = [buf(f"chunk{u}", [P, NSCAN, c]) for u in range(1 if running else 2)]
        kraw, sqr, vb, kn, kbn, kw = (buf(n, [P, HG, P]) for n in ("kraw", "sqr", "vb", "kn", "kbn", "kw"))
        o = kraw if running else buf("o", [P, HG, P])
        vn, res, on = kbn, sqr, sqr
        qsq, kT, kbT, dec, AT, qkT, T_, TT_, X = (
            buf(n, [P, HG, c]) for n in ("qsq", "kT", "kbT", "dec", "AT", "qkT", "T", "TT", "X"))
        mat = buf("mat", [P, 2, HG, c])
        ss, rs, lg, be = buf("ss", [P, 3, HG]), buf("rs", [P, 2, 2, HG]), buf("lg", [P, 3, HG]), buf("os", [P, 2, HG])
        ors = buf("ors", [P, HG])
        xdt, wx, y = (buf(n, [P, HS, PS]) for n in ("xdt", "wx", "y"))
        tmp = buf("tmp", [P, XG])
        btok, cbs = buf("btok", [P, G, P]), buf("cb", [P, G, c])
        sdec, wg = buf("sdec", [P, 2, 4, c]), buf("wg", [P, 2, 4, c])
        yss = buf("yss", [P, 4, G])
        drow, snw, gnw = buf("drow", [P, HS]), buf("snw", [P, ZT]), buf("gnw", [P, 1])
        S = buf("S", [P, nseq, HG, P])
        if running:
            hb_ = buf("h", [P, HPL, NB, XG])
            cm, km, qm = buf("cm", [P, NB, G, c]), buf("km", [P, NB, HG, c]), buf("qm", [P, NB, HG, c])
            bm, kwm = buf("bm", [P, 2, P]), buf("kwm", [P, 2, NHB, P])
        else:
            h = buf("h", [P, HS, PS])
        ps = ctx.enter_context(nc.psum_tensor(f"{tag}_ps", [P, 8, 512], F32))

        def bank(n, m, w):
            return ps[:, n, 0:m * w].rearrange("p (m w) -> p m w", w=w)

        def cut(ap, l, late_half):
            s = 2 << l
            if s == 64:
                return ap[:, :, 64:c] if late_half else ap[:, :, 0:64]
            if s == 32 and late_half:
                return ap[:, :, 32:c]
            if s == 32:
                return ap[:, :, 0:96].rearrange("p h (b s) -> p h b s", s=32)[:, :, 0::2, :]
            whole = ap[:, :, 0:c // (2 * s) * 2 * s].rearrange("p h (b s) -> p h b s", s=2 * s)
            return whole[:, :, :, s:] if late_half else whole[:, :, :, 0:s]

        def top(l):
            return 64 if l == 5 else c

        def cut_bank(n, l, late_half):
            return cut(bank(n, NHB, c)[0:c], l, late_half)

        A, B, E_ = (0, 1), (2, 3), (4, 5, 6, 7)

        def E(name, per=1):
            return Event(nc, f"{tag}_{name}", per)

        nl = levels - 1
        loaded = Loads(nc, f"{tag}_loaded", len(cd))
        stored = Loads(nc, f"{tag}_stored", len(cd))
        consts_in = Loads(nc, f"{tag}_consts_in", 1, 3)
        state_in, state_out = Loads(nc, f"{tag}_S_in", 1), Loads(nc, f"{tag}_S_out", 1, NB // 2 if running else 1)
        h_in, h_out = Loads(nc, f"{tag}_h_in", HPL), Loads(nc, f"{tag}_h_out", HPL)
        zeroed = E("zeroed", 1)
        m_k, m_v, m_qss, m_seg, m_kT, m_kbT = E("m_k", 2), E("m_v", 2), E("m_qss"), E("m_seg", 2), E("m_kT", 2), E("m_kbT", 2)
        m_G, m_QK, m_T, m_X, m_dT, m_dTT = (E("m_G", 2), E("m_QK", 2), E("m_T", 2), E("m_X", 2 * nl),
                                            E("m_dT", 2 * (nl - 1)), E("m_dTT", 2 * nl))
        m_KS, m_VN, m_QS, m_AV, m_SU, m_oT = (E("m_KS", 2), E("m_VN", 2), E("m_QS", 2), E("m_AV", 2),
                                              E("m_SU", 2 * nseq), E("m_oT", 2))
        m_x, m_B, m_CB, m_sseg, m_in, m_inter, m_h, m_z, m_yT = (
            E("m_x", 4), E("m_B"), E("m_CB"), E("m_sseg", 8), E("m_in", 4), E("m_inter", 4), E("m_h", 4 * nseq),
            E("m_z", 4), E("m_yT", 4))
        a_qsq, a_k, a_ksq, a_ln, a_rs, a_kT, a_kbT, a_dec = (
            E("a_qsq"), E("a_k", 2), E("a_ksq"), E("a_ln"), E("a_rs"), E("a_kT", 2), E("a_kbT", 2), E("a_dec", 2))
        a_T, a_X, a_vn, a_osq, a_oln, a_ors = E("a_T", 2), E("a_X", 2 * nl), E("a_vn", 2), E("a_osq"), E("a_oln"), E("a_ors")
        a_B, a_cb, a_sdec, a_ysq, a_yln, a_yrs, a_x, a_yn = (E("a_B"), E("a_cb"), E("a_sdec", 8), E("a_ysq", 4), E("a_yln"),
                                                        E("a_yrs"), E("a_x", 4), E("a_yn", 4))
        v_vb, v_kss, v_ss, v_kn, v_kbn, v_AT, v_qk, v_TT, v_T, v_TTn = (
            E("v_vb", 2), E("v_kss"), E("v_ss", 2), E("v_kn"), E("v_kbn"), E("v_AT", 2), E("v_qk", 2), E("v_TT", 2),
            E("v_T", 2 * (nl - 1)), E("v_TTn", 2 * nl))
        v_res, v_o1, v_o2, v_S0, v_S1, v_oq, v_oss, v_oms, v_on, v_yg = (
            E("v_res", HG), E("v_o1", 2), E("v_o2", 2), E("v_S0", nseq), E("v_S1", 2 * nseq), E("v_oq"), E("v_oss"),
            E("v_oms"), E("v_on"), E("v_yg", 2))
        v_xdt, v_wg, v_y1, v_tmp, v_y2, v_h0, v_h1, v_yz, v_yms, v_ys = (
            E("v_xdt", 4), E("v_wg", 8), E("v_y1", 4), E("v_tmp", 4), E("v_y2", 4), E("v_h0", 4),
            E("v_h1", 4 * nseq), E("v_yz", 4), E("v_yms"), E("v_ys", 4))
        v_rq = E("v_rq")
        v_cm, v_km, v_qm = E("v_cm"), E("v_km"), E("v_qm")
        p_y0 = E("p_y0", 4)
        p_kw, p_mat, p_wx, p_bm, p_kwm = E("p_kw"), E("p_mat", 2 * levels), E("p_wx", 4), E("p_bm", 4 * NB), E("p_kwm", 2 * NB)
        block = ctx.enter_context(nc.Block())

        def chunks(eng, body):
            if running:
                body(NC, 0, 0, True, True)
                return
            body(0, 0, 0, True, False)
            with eng.Fori(0, NC // 2 - 1) as i:
                for n in (1, 2):
                    body(2 * i + n, n % 2, 2 * i + n, False, False)
            body(NC - 1, 1, NC - 1, False, True)

        last_place, last_round = (0, 0) if running else (1, NC - 1)

        def at(tile, t, n=c):
            return tab[tile][0:n, bass.ds(t, 1), :].rearrange("p a m -> p (a m)")

        def decay(t, lo_, hi_):
            return tab["EL"][:, NC:NC + NB, lo_:hi_] if running else tab["EL"][:, bass.ds(t, 1), lo_:hi_]

        @block.sync
        def _(sp):
            sp.dma_start(drow[:, :], d["ssm_d"].to_broadcast([P, HS])).then_inc(consts_in.sems[0], 16)
            sp.dma_start(snw[:, :], d["ssm_norm"]).then_inc(consts_in.sems[0], 16)
            sp.dma_start(gnw[:, :], d["gdn_norm"]).then_inc(consts_in.sems[0], 16)
            if running:
                sp.dma_start(cd[0][:, :, :], scratch[0:NSCAN, :, TP:T].rearrange("m p n -> p m n")).then_inc(loaded.sems[0], 16)
                def load_h(g):
                    sp.dma_start(hb_[:, g % HPL, :, :], d["ssm_old"][:, :, g * XG:(g + 1) * XG].rearrange(
                        "b p n -> p b n")).then_inc(h_in.sems[g % HPL], 16)

                load_h(0)
                sp.dma_start(S[:, :, :, :].rearrange("p b h v -> p b (h v)"),
                             d["gdn_old"].rearrange("b p n -> p b n")).then_inc(state_in.sems[0], 16)
                for g in range(1, HPL):
                    load_h(g)
                for g in range(G):
                    sp.wait_ge(v_h1.sem, v_h1.at(0, NB * (g + 1)))
                    sp.dma_start(d["ssm_new"][1:, :, g * XG:(g + 1) * XG].rearrange("b p n -> p b n"),
                                 hb_[:, g % HPL, :, :]).then_inc(h_out.sems[g % HPL], 16)
                    if g + HPL < G:
                        sp.wait_ge(h_out.sems[g], h_out.at(0))
                        load_h(g + HPL)
                for b in range(0, NB, 2):
                    sp.wait_ge(v_S1.sem, v_S1.at(0, 2 * (b + 2)))
                    sp.dma_start(d["gdn_new"][1 + b:3 + b].rearrange("b p n -> p b n"),
                                 S[:, b:b + 2, :, :].rearrange("p b h v -> p b (h v)")).then_inc(state_out.sems[0], 16)
                sp.wait_ge(v_yg.sem, v_yg.at(0))
                sp.wait_ge(v_ys.sem, v_ys.at(0))
                sp.dma_start(mixed[:, :, TP:T].rearrange("m p n -> p m n"), cd[0][:, XT + GT:, :]).then_inc(stored.sems[0], 16)
                for g in range(HPL):
                    sp.wait_ge(h_out.sems[g], h_out.at((G - 1 - g) // HPL))
            else:
                def load(t, u):
                    sp.dma_start(cd[u][:, :, :], scratch[0:NSCAN, :, bass.ds(t * C, C)].rearrange(
                        "m p n -> p m n")).then_inc(loaded.sems[u], 16)

                def store(t, u):
                    sp.wait_ge(v_yg.sem, v_yg.at(t))
                    sp.wait_ge(v_ys.sem, v_ys.at(t))
                    sp.dma_start(mixed[:, :, bass.ds(t * C, C)].rearrange("m p n -> p m n"),
                                           cd[u][:, XT + GT:, :]).then_inc(stored.sems[u], 16)

                for u in range(2):
                    load(u, u)
                with sp.Fori(0, NC // 2 - 1) as i:
                    for u in range(2):
                        store(2 * i + u, u)
                        sp.wait_ge(stored.sems[u], stored.at(i))
                        load(2 * i + u + 2, u)
                for u in range(2):
                    store(NC - 2 + u, u)
                sp.wait_ge(v_S1.sem, v_S1.at(NC - 1))
                sp.wait_ge(v_h1.sem, v_h1.at(NC - 1))
                sp.dma_start(d["gdn_new"][0], S[:, 0, :, :].rearrange("p h v -> p (h v)")).then_inc(state_out.sems[0], 16)
                sp.dma_start(d["ssm_new"][0], h[:, :, :].rearrange("p h v -> p (h v)")).then_inc(h_out.sems[0], 16)
                sp.wait_ge(h_out.sems[0], h_out.at(0))
                sp.wait_ge(stored.sems[1], stored.at(NC // 2 - 1))
            sp.wait_ge(stored.sems[0], stored.at(0 if running else NC // 2 - 1))
            sp.wait_ge(state_out.sems[0], state_out.at(0))

        @block.tensor
        def _(pe):
            prime(pe, m_sseg, m_inter, m_in, m_h, m_z, m_k, m_x, m_v, m_B, m_CB, m_qss, m_seg, m_kT, m_kbT, m_G,
                  m_QK, m_T, m_X, m_dT, m_dTT, m_KS, m_VN, m_QS, m_AV, m_SU, m_yT, m_oT)
            ident = con["ident"]

            def turn(place, bk, tile):
                for k in range(4):
                    ins = pe.transpose(ps[0:c, bk, k * P:(k + 1) * P], cd[place][:, tile + k, :], ident[:, :])
                return ins

            def k_in(u, r):
                pe.wait_ge(loaded.sems[u], 8 * (r - u) + 16 if not running else 16)
                for hb in range(2):
                    turn(u, E_[hb], 32 + 4 * hb).then_inc(m_k.sem, 1)

            def q_sizes(r):
                pe.wait_ge(a_qsq.sem, a_qsq.at(r))
                for hd in range(HG):
                    ins = pe.matmul(ps[0:c, E_[2], hd:hd + 1], qsq[:, hd, :], con["ones"][:, 0:1], start=True, stop=True)
                ins.then_inc(m_qss.sem, 1)

            def turn_out(r):
                for hb in range(2):
                    transpose_bank(pe, ps[:, A[hb], :], [on[0:c, NHB * hb + n, :] for n in range(NHB)], c, ident).then_inc(m_oT.sem, 1)

            def body(t, u, r, first, last):
                ch = cd[u]

                def decays(bk, heads):
                    tok = bass.ds(t * C, c)
                    for n, hd in enumerate(heads):
                        out = bank(bk, 4, c)[0:c, n, :]
                        sel = con["selT"][0:3 * H, hd, 0:c]
                        pe.matmul(out, sel, tab["accT"][0:3 * H, tok], start=True, stop=False)
                        pe.matmul(out, tab["naccT"][0:3 * H, tok], sel, start=False, stop=False)
                        ins = pe.matmul(out, con["identb"][0:c, 0:c], late[0:c, 0:c], start=False, stop=True)
                    return ins

                def ssd_decays(g, half):
                    n = 2 * g + half
                    if n >= 2:
                        pe.wait_ge(a_sdec.sem, a_sdec.at(r, n - 1))
                    else:
                        first = a_cb if half else a_B
                        pe.wait_ge(first.sem, first.at(r))
                    decays(E_[half], [g * HPG + 4 * half + k for k in range(4)]).then_inc(m_sseg.sem, 1)

                def ssd_inter(g):
                    if g:
                        pe.wait_ge(v_yz.sem, v_yz.at(r, g))
                        pe.wait_ge(v_h1.sem, v_h1.ahead(r))
                    else:
                        pe.wait_ge(v_xdt.sem, v_xdt.at(r))
                        pe.wait_ge(a_x.sem, a_x.at(r))
                        pe.wait_ge(v_h1.sem, v_h1.ahead(r))
                    if running:
                        pe.wait_ge(h_in.sems[g % HPL], h_in.at(g // HPL))
                        pe.wait_ge(v_cm.sem, v_cm.at(0))
                        for b in range(NB):
                            ins = pe.matmul(ps[0:c, E_[3], :], cm[:, b, g, :], hb_[:, g % HPL, b, :],
                                            start=(b == 0), stop=(b == NB - 1))
                    else:
                        ins = pe.matmul(ps[0:c, E_[3], :], ch[:, 20 + g, :], h[:, g * HPG:(g + 1) * HPG, :].rearrange(
                            "p h v -> p (h v)"), start=True, stop=True)
                    ins.then_inc(m_inter.sem, 1)

                def ssd_inside(g):
                    if g:
                        pe.wait_ge(v_h1.sem, v_h1.at(r, nseq * g))
                    else:
                        pe.wait_ge(v_xdt.sem, v_xdt.at(r))
                    for half in range(2):
                        pe.wait_ge(v_wg.sem, v_wg.at(r, 2 * g + half + 1))
                        for k in range(4):
                            ins = pe.matmul(ps[0:c, E_[2], (4 * half + k) * PS:(4 * half + k + 1) * PS],
                                            wg[0:c, half, k, :], xdt[0:c, g * HPG + 4 * half + k, :],
                                            start=True, stop=True)
                    ins.then_inc(m_in.sem, 1)

                def ssd_rest(g):
                    pe.wait_ge(v_tmp.sem, v_tmp.at(r, g + 1))
                    turn_in(E_[3], XT + GT + 4 * g).then_inc(m_z.sem, 1)
                    if g < 3:
                        ssd_decays(g + 1, 0)
                        ssd_decays(g + 1, 1)
                    pe.wait_ge(p_wx.sem, p_wx.at(r, g + 1))
                    pe.wait_ge(a_B.sem, a_B.at(r))
                    pe.wait_ge(v_y1.sem, v_y1.at(r, g + 1))
                    for b in range(nseq):
                        if running:
                            pe.wait_ge(p_bm.sem, p_bm.at(0, NB * g + b + 1))
                            if b >= 2:
                                pe.wait_ge(v_h1.sem, v_h1.at(0, NB * g + b - 1))
                            elif b and g + 1 < G:
                                pe.wait_ge(a_sdec.sem, a_sdec.at(0, 2 * g + 3))
                        lhs = bm[0:c, b % 2, :] if running else btok[0:c, g, :]
                        pe.matmul(ps[:, E_[2 - 2 * (b % 2)], :], lhs, wx[0:c, g * HPG:(g + 1) * HPG, :].rearrange(
                            "p h v -> p (h v)"), start=True, stop=True).then_inc(m_h.sem, 1)

                def turn_in(bk, tile):
                    return turn(u, bk, tile)

                def four(bk, hb, w, lhs, rhs):
                    for n in range(NHB):
                        hd = NHB * hb + n
                        l, m = lhs(hd), rhs(hd)
                        ins = pe.matmul(ps[0:l.shape[1], bk, n * w:(n + 1) * w], l, m, start=True, stop=True)
                    return ins

                pe.wait_ge(loaded.sems[u], 8 * (r - u) + 16 if not running else 16)
                pe.wait_ge(v_o2.sem, v_o2.ahead(r))
                for hb in range(2):
                    decays(A[hb], [HS + NHB * hb + n for n in range(NHB)]).then_inc(m_seg.sem, 1)
                pe.wait_ge(v_S1.sem, v_S1.ahead(r))
                for hb in range(2):
                    turn_in(B[hb], 40 + 4 * hb).then_inc(m_v.sem, 1)
                for g in range(G):
                    if first:
                        pe.wait_ge(a_k.sem, a_k.at(r))
                        pe.wait_ge(v_ss.sem, v_ss.at(r))
                    else:
                        pe.wait_ge(v_ys.sem, v_ys.at(r - 1, g + 1))
                    turn_in(E_[g], 4 * g).then_inc(m_x.sem, 1)
                pe.wait_ge(v_xdt.sem, v_xdt.at(r, 1))
                pe.wait_ge(a_x.sem, a_x.at(r, 1))
                turn_in(E_[0], 16).then_inc(m_B.sem, 1)
                pe.wait_ge(v_xdt.sem, v_xdt.at(r, 2))
                pe.wait_ge(a_x.sem, a_x.at(r, 2))
                for g in range(G):
                    ins = pe.matmul(bank(E_[1], G, c)[0:c, g, :], ch[:, 16 + g, :], ch[:, 20 + g, :],
                                    start=True, stop=True)
                ins.then_inc(m_CB.sem, 1)
                ssd_decays(0, 0)
                ssd_decays(0, 1)
                pe.wait_ge(v_kn.sem, v_kn.at(r))
                for hb in range(2):
                    pe.wait_ge(a_dec.sem, a_dec.at(r, hb + 1))
                    transpose_bank(pe, ps[:, A[hb], :], [kn[0:c, NHB * hb + n, :] for n in range(NHB)], c, ident).then_inc(m_kT.sem, 1)
                pe.wait_ge(v_kbn.sem, v_kbn.at(r))
                pe.wait_ge(v_vb.sem, v_vb.at(r))
                for hb in range(2):
                    transpose_bank(pe, ps[:, B[hb], :], [kbn[0:c, NHB * hb + n, :] for n in range(NHB)], c, ident).then_inc(m_kbT.sem, 1)
                for hb in range(2):
                    pe.wait_ge(a_kT.sem, a_kT.at(r, hb + 1))
                    pe.wait_ge(a_kbT.sem, a_kbT.at(r, hb + 1))
                    four(B[hb], hb, c, lambda n: kT[:, n, :], lambda n: kbT[:, n, :]).then_inc(m_G.sem, 1)
                for hb in range(2):
                    four(A[hb], hb, c, lambda n: kT[:, n, :], lambda n: ch[:, 24 + n, :]).then_inc(m_QK.sem, 1)
                ssd_inter(0)
                ssd_inside(0)
                if not first:
                    pe.wait_ge(v_on.sem, v_on.ahead(r))
                    pe.wait_ge(v_qk.sem, v_qk.at(r))
                    turn_out(r - 1)
                for hb in range(2):
                    pe.wait_ge(v_TT.sem, v_TT.at(r, hb + 1))
                    transpose_bank(pe, ps[:, B[hb], :], [TT_[0:c, NHB * hb + n, :] for n in range(NHB)], c, ident).then_inc(m_T.sem, 1)
                ssd_rest(0)
                pe.wait_ge(v_yg.sem, v_yg.ahead(r))
                for l in range(nl):
                    g = l + 1 if not running else None
                    for hb in range(2):
                        n = 2 * l + hb
                        pe.wait_ge(p_mat.sem, p_mat.at(r, n + 3))
                        if l == 0:
                            pe.wait_ge(v_qk.sem, v_qk.at(r, hb + 1))
                            pe.wait_ge(a_T.sem, a_T.at(r, hb + 1))
                        else:
                            pe.wait_ge(v_T.sem, v_T.at(r, n - 1))
                            pe.wait_ge(v_TTn.sem, v_TTn.at(r, n - 1))
                        four(A[hb], hb, c, lambda n: mat[0:c, (l + 1) % 2, n, :], lambda n: T_[0:c, n, :]).then_inc(m_X.sem, 1)
                    if l < 3 and not running:
                        ssd_inter(g)
                    if l == 3 and not last:
                        pe.wait_ge(a_sdec.sem, a_sdec.at(r))
                        k_in(1 - u, r + 1)
                    if l == 4 and not last:
                        pe.wait_ge(v_h1.sem, v_h1.at(r))
                        q_sizes(r + 1)
                    for hb in range(2):
                        pe.wait_ge(a_X.sem, a_X.at(r, 2 * l + hb + 1))
                        if l < nl - 1:
                            four(B[hb], hb, c, lambda n: TT_[0:c, n, :], lambda n: X[0:c, n, :]).then_inc(m_dT.sem, 1)
                        four(A[hb], hb, c, lambda n: X[0:c, n, 0:top(l)], lambda n: TT_[0:c, n, :]).then_inc(m_dTT.sem, 1)
                    if not running and l < 3:
                        ssd_inside(g)
                        ssd_rest(g)
                if running:
                    for g in range(1, G):
                        ssd_inter(g)
                        ssd_inside(g)
                        ssd_rest(g)
                if running:
                    pe.wait_ge(state_in.sems[0], state_in.at(0))
                    pe.wait_ge(v_km.sem, v_km.at(0))
                    pe.wait_ge(v_qm.sem, v_qm.at(0))
                pe.wait_ge(v_S1.sem, v_S1.ahead(r))
                pe.wait_ge(zeroed.sem, zeroed.at(0))

                def with_state(bk, hb, plain, masked):
                    for n in range(NHB):
                        hd = NHB * hb + n
                        for b in range(nseq):
                            ins = pe.matmul(ps[0:c, bk, n * P:(n + 1) * P], masked[:, b, hd, :] if running else plain(hd),
                                            S[:, b, hd, :], start=(b == 0), stop=(b == nseq - 1))
                    return ins

                for hb in range(2):
                    if nl > 1:
                        pe.wait_ge(v_T.sem, v_T.at(r, 2 * (nl - 1) - 1 + hb))
                    with_state(B[hb], hb, lambda n: kT[:, n, :], km if running else None).then_inc(m_KS.sem, 1)
                for hb in range(2):
                    pe.wait_ge(v_res.sem, v_res.at(r, NHB * (hb + 1)))
                    pe.wait_ge(v_TTn.sem, v_TTn.at(r, 2 * nl - 1 + hb))
                    four(A[hb], hb, P, lambda n: TT_[0:c, n, :], lambda n: res[0:c, n, :]).then_inc(m_VN.sem, 1)
                for hb in range(2):
                    with_state(B[hb], hb, lambda n: ch[:, 24 + n, :], qm if running else None).then_inc(m_QS.sem, 1)
                for hb in range(2):
                    pe.wait_ge(a_vn.sem, a_vn.at(r, hb + 1))
                    four(A[hb], hb, P, lambda n: qkT[0:c, n, :], lambda n: vn[0:c, n, :]).then_inc(m_AV.sem, 1)
                for b in range(nseq):
                    for hb in range(2):
                        n = 2 * b + hb
                        if b == 0:
                            pe.wait_ge(v_o1.sem, v_o1.at(r, hb + 1))
                            pe.wait_ge(p_kw.sem, p_kw.at(r))
                        else:
                            pe.wait_ge(v_S1.sem, v_S1.at(r, n - 1))
                        if running:
                            pe.wait_ge(p_kwm.sem, p_kwm.at(0, n + 1))
                        four(B[hb], hb, P, lambda m: kwm[0:c, n % 2, m % NHB, :] if running else kw[0:c, m, :],
                                     lambda m: vn[0:c, m, :]).then_inc(m_SU.sem, 1)
                for g in range(G):
                    pe.wait_ge(a_yn.sem, a_yn.at(r, g + 1))
                    if g == 3:
                        pe.wait_ge(v_yz.sem, v_yz.at(r))
                    if g == 2:
                        pe.wait_ge(v_h1.sem, v_h1.at(r))
                        if not last:
                            pe.wait_ge(v_ss.sem, v_ss.at(r + 1, 1))
                    if g < 2 and not last:
                        pe.wait_ge(a_k.sem, a_k.at(r + 1, g + 1))
                    transpose_bank(pe, ps[:, E_[g], :], [
                        y[0:c, g * HPG + 2 * n:g * HPG + 2 * n + 2, :].rearrange("p h v -> p (h v)")
                        for n in range(4)], c, ident).then_inc(m_yT.sem, 1)

            k_in(0, 0)
            q_sizes(0)
            chunks(pe, body)
            pe.wait_ge(v_on.sem, v_on.at(last_round))
            pe.wait_ge(v_o2.sem, v_o2.at(last_round))
            turn_out(last_round)

        @block.scalar
        def _(act):
            prime(act, a_sdec, a_qsq, a_ksq, a_B, a_cb, a_ln, a_rs, a_dec, a_ysq, a_yln, a_yrs, a_x, a_yn, a_osq, a_oln,
                  a_ors, a_k, a_kT, a_kbT, a_T, a_X, a_vn)
            act.activation(lg[:, 0, 0:1], con["ones"][:, 0:1], ACT.Ln)

            act.wait_ge(zeroed.sem, zeroed.at(0))

            def k_and_q(u, r):
                act.wait_ge(loaded.sems[u], 8 * (r - u) + 16 if not running else 16)
                for hb in range(2):
                    act.wait_ge(m_k.sem, m_k.at(r, hb + 1))
                    act.wait_ge(v_kn.sem, v_kn.ahead(r))
                    act.activation(kraw[0:c, NHB * hb:NHB * hb + NHB, :], bank(E_[hb], NHB, P)[0:c], ACT.Copy).then_inc(a_k.sem, 1)
                act.wait_ge(m_qss.sem, m_qss.ahead(r))
                act.activation(qsq[:, :, :], cd[u][:, 24:32, :], ACT.Square).then_inc(a_qsq.sem, 1)

            def k_squares(r):
                act.wait_ge(a_k.sem, a_k.at(r))
                if not isinstance(r, int) or r:
                    act.wait_ge(m_oT.sem, m_oT.ahead(r - 1))
                act.activation(sqr[0:c, :, :], kraw[0:c, :, :], ACT.Square).then_inc(a_ksq.sem, 1)

            def kq_log(r):
                act.wait_ge(v_ss.sem, v_ss.at(r))
                act.activation(lg[0:c, 0:2, :], ss[0:c, 0:2, :], ACT.Ln).then_inc(a_ln.sem, 1)

            def kq_scale(u, r):
                act.wait_ge(a_ln.sem, a_ln.at(r))
                act.activation(rs[0:c, u, :, :], lg[0:c, 0:2, :], ACT.Exp, scale=-0.5).then_inc(a_rs.sem, 1)

            def out_scale(r):
                act.wait_ge(v_oms.sem, v_oms.at(r))
                act.activation(lg[0:c, 2, :], ss[0:c, 2, :], ACT.Ln).then_inc(a_oln.sem, 1)
                act.wait_ge(a_oln.sem, a_oln.at(r))
                act.activation(ors[0:c, :], lg[0:c, 2, :], ACT.Exp, scale=-0.5).then_inc(a_ors.sem, 1)

            def body(t, u, r, first, last):
                ch = cd[u]

                def copy4(out, bk, ev, w):
                    act.activation(out, bank(bk, NHB, w)[0:out.shape[0]], ACT.Copy).then_inc(ev.sem, 1)

                def ssd_decay(g):
                    for half in range(2):
                        n = 2 * g + half
                        act.wait_ge(m_sseg.sem, m_sseg.at(r, n + 1))
                        if n >= 2:
                            act.wait_ge(v_wg.sem, v_wg.at(r, n - 1))
                        else:
                            act.wait_ge(v_wg.sem, v_wg.ahead(r))
                        act.activation(sdec[0:c, half, :, :], bank(E_[half], 4, c)[0:c], ACT.Exp).then_inc(a_sdec.sem, 1)

                for hb in range(2):
                    act.wait_ge(m_seg.sem, m_seg.at(r, hb + 1))
                    act.wait_ge(v_qk.sem, v_qk.ahead(r))
                    act.activation(dec[0:c, NHB * hb:NHB * hb + NHB, :], bank(A[hb], NHB, c)[0:c], ACT.Exp).then_inc(a_dec.sem, 1)
                for g in range(G):
                    act.wait_ge(v_xdt.sem, v_xdt.at(r, g + 1))
                    act.wait_ge(m_yT.sem, m_yT.ahead(r))
                    act.activation(y[0:c, g * HPG:(g + 1) * HPG, :], bank(E_[g], HPG, PS)[0:c], ACT.Copy).then_inc(a_x.sem, 1)
                act.wait_ge(m_B.sem, m_B.at(r))
                act.wait_ge(m_h.sem, m_h.ahead(r))
                act.activation(btok[0:c, :, :], bank(E_[0], G, P)[0:c], ACT.Copy).then_inc(a_B.sem, 1)
                act.wait_ge(m_CB.sem, m_CB.at(r))
                act.wait_ge(v_wg.sem, v_wg.ahead(r))
                act.activation(cbs[0:c, :, :], bank(E_[1], G, c)[0:c], ACT.Copy).then_inc(a_cb.sem, 1)
                ssd_decay(0)
                for hb in range(2):
                    act.wait_ge(m_kT.sem, m_kT.at(r, hb + 1))
                    act.wait_ge(m_KS.sem, m_KS.ahead(r))
                    copy4(kT[:, NHB * hb:NHB * hb + NHB, :], A[hb], a_kT, c)
                for hb in range(2):
                    act.wait_ge(m_kbT.sem, m_kbT.at(r, hb + 1))
                    copy4(kbT[:, NHB * hb:NHB * hb + NHB, :], B[hb], a_kbT, c)
                if not first:
                    out_scale(r - 1)
                ssd_decay(1)
                for hb in range(2):
                    act.wait_ge(m_T.sem, m_T.at(r, hb + 1))
                    copy4(T_[0:c, NHB * hb:NHB * hb + NHB, :], B[hb], a_T, c)
                for l in range(nl):
                    for hb in range(2):
                        act.wait_ge(m_X.sem, m_X.at(r, 2 * l + hb + 1))
                        if l:
                            act.wait_ge(m_dTT.sem, m_dTT.at(r, 2 * l - 1 + hb))
                        else:
                            act.wait_ge(m_dTT.sem, m_dTT.ahead(r))
                        copy4(X[0:c, NHB * hb:NHB * hb + NHB, :], A[hb], a_X, c)
                    if not running and l < 2:
                        ssd_decay(l + 2)
                    if l == 3 and not last:
                        k_and_q(1 - u, r + 1)
                    if l == 4 and not last:
                        k_squares(r + 1)
                if running:
                    ssd_decay(2)
                    ssd_decay(3)
                for g in range(G):
                    act.wait_ge(v_yz.sem, v_yz.at(r, g + 1))
                    if g:
                        act.wait_ge(a_ysq.sem, a_ysq.at(r, g))
                    act.wait_ge(v_tmp.sem, v_tmp.at(r))
                    act.wait_ge(v_y2.sem, v_y2.at(r))
                    act.activation(tmp[0:c, :], y[0:c, g * HPG:(g + 1) * HPG, :].rearrange("p h v -> p (h v)"),
                                            ACT.Square, accum_out=yss[0:c, 0, g:g + 1]).then_inc(a_ysq.sem, 1)
                if not last:
                    kq_log(r + 1)
                act.wait_ge(v_yms.sem, v_yms.at(r))
                act.activation(yss[0:c, 2, :], yss[0:c, 1, :], ACT.Ln).then_inc(a_yln.sem, 1)
                act.wait_ge(a_yln.sem, a_yln.at(r))
                act.activation(yss[0:c, 3, :], yss[0:c, 2, :], ACT.Exp, scale=-0.5).then_inc(a_yrs.sem, 1)
                if not last:
                    kq_scale(1 - u, r + 1)
                for hb in range(2):
                    act.wait_ge(m_VN.sem, m_VN.at(r, hb + 1))
                    copy4(vn[0:c, NHB * hb:NHB * hb + NHB, :], A[hb], a_vn, P)
                act.wait_ge(a_yrs.sem, a_yrs.at(r))
                for g in range(G):
                    yg = y[0:c, g * HPG:(g + 1) * HPG, :]
                    act.activation(yg, yg, ACT.Copy, scale=yss[0:c, 3, g:g + 1]).then_inc(a_yn.sem, 1)
                act.wait_ge(v_oq.sem, v_oq.at(r))
                act.wait_ge(m_VN.sem, m_VN.at(r))
                act.activation(sqr[0:c, :, :], o[0:c, :, :], ACT.Square).then_inc(a_osq.sem, 1)

            k_and_q(0, 0)
            k_squares(0)
            kq_log(0)
            kq_scale(0, 0)
            chunks(act, body)
            out_scale(last_round)

        @block.vector
        def _(dve):
            prime(dve, zeroed, v_wg, v_tmp, v_y1, v_h0, v_y2, v_h1, v_yz, v_xdt, v_cm, v_qm, v_vb, v_ss,
                  v_kss, v_kn, v_kbn, v_AT, v_qk, v_TT, v_km, v_T, v_TTn, v_yms, v_res, v_o1, v_S0, v_o2,
                  v_S1, v_rq, v_oq, v_oss, v_oms, v_on, v_ys, v_yg)
            dve.memset(ss[:, :, :], 1.0)
            if not running:
                dve.memset(S[:, :, :, :], 0.0)
                dve.memset(h[:, :, :], 0.0).then_inc(zeroed.sem, 1)
            else:
                dve.memset(tmp[:, 0:1], 0.0).then_inc(zeroed.sem, 1)
            dve.wait_ge(consts_in.sems[0], consts_in.at(0))
            dve.wait_ge(zeroed.sem, zeroed.at(0))

            def heads(hb):
                return slice(NHB * hb, NHB * hb + NHB)

            def kq_sizes(r):
                dve.wait_ge(m_qss.sem, m_qss.at(r))
                dve.tensor_scalar(ss[0:c, 1, :], ps[0:c, E_[2], 0:HG], EPS, None, ALU.add).then_inc(v_ss.sem, 1)
                dve.wait_ge(a_ksq.sem, a_ksq.at(r))
                dve.tensor_reduce(be[0:c, 0, :], sqr[0:c, :, :], AX, ALU.add).then_inc(v_kss.sem, 1)
                dve.wait_ge(v_kss.sem, v_kss.at(r))
                dve.tensor_scalar(ss[0:c, 0, :], be[0:c, 0, :], EPS, None, ALU.add).then_inc(v_ss.sem, 1)

            def scale_k(u, r):
                dve.wait_ge(a_rs.sem, a_rs.at(r))
                dve.wait_ge(m_kT.sem, m_kT.ahead(r))
                dve.wait_ge(p_kw.sem, p_kw.ahead(r))
                dve.wait_ge(v_kbn.sem, v_kbn.ahead(r))
                dve.tensor_tensor(kn[0:c, :, :], kraw[0:c, :, :], bcast(rs[0:c, u, 0, :], P), ALU.mult).then_inc(v_kn.sem, 1)

            def mean_square(r):
                dve.wait_ge(a_osq.sem, a_osq.at(r))
                dve.tensor_reduce(be[0:c, 1, :], sqr[0:c, :, :], AX, ALU.add).then_inc(v_oss.sem, 1)
                dve.wait_ge(v_oss.sem, v_oss.at(r))
                dve.tensor_scalar(ss[0:c, 2, :], be[0:c, 1, :], 1.0 / P, EPS, ALU.mult, ALU.add).then_inc(v_oms.sem, 1)

            def normalise(r):
                dve.wait_ge(v_oq.sem, v_oq.at(r))
                dve.wait_ge(a_ors.sem, a_ors.at(r))
                dve.tensor_tensor(on[0:c, :, :], o[0:c, :, :], bcast(ors[0:c, :], P), ALU.mult).then_inc(v_on.sem, 1)

            def gate_out(r, place):
                for hb in range(2):
                    gate = cd[place][:, XT + GT + ZT + NHB * hb:XT + GT + ZT + NHB * hb + NHB, :]
                    dve.wait_ge(m_oT.sem, m_oT.at(r, hb + 1))
                    dve.scalar_tensor_tensor(out=gate, in0=bank(A[hb], NHB, c), scalar=gnw[:, 0:1], in1=gate,
                                             op0=ALU.mult, op1=ALU.mult).then_inc(v_yg.sem, 1)

            def body(t, u, r, first, last):
                ch = cd[u]

                def group(buf_, g):
                    return buf_[0:c, g * HPG:(g + 1) * HPG, :]

                def ssd_weights(g):
                    for half in range(2):
                        n = 2 * g + half
                        dve.wait_ge(a_sdec.sem, a_sdec.at(r, n + 1))
                        if g:
                            dve.wait_ge(m_in.sem, m_in.at(r, g))
                        else:
                            dve.wait_ge(a_cb.sem, a_cb.at(r))
                            dve.wait_ge(m_in.sem, m_in.ahead(r))
                        dve.tensor_tensor(wg[0:c, half, :, :], sdec[0:c, half, :, :], bmid(cbs[0:c, g, :], 4),
                                                  ALU.mult).then_inc(v_wg.sem, 1)

                def ssd_group(g):
                    dve.wait_ge(m_inter.sem, m_inter.at(r, g + 1))
                    if g:
                        dve.wait_ge(v_y2.sem, v_y2.at(r, g))
                    else:
                        dve.wait_ge(a_ysq.sem, a_ysq.ahead(r))
                    dve.tensor_tensor(tmp[0:c, :].rearrange("p (h v) -> p h v", v=PS), bank(E_[3], HPG, PS)[0:c],
                                               bcast(at("E", t)[:, g * HPG:(g + 1) * HPG], PS), ALU.mult).then_inc(v_tmp.sem, 1)
                    dve.wait_ge(m_in.sem, m_in.at(r, g + 1))
                    dve.wait_ge(p_y0.sem, p_y0.at(r, g + 1))
                    dve.tensor_tensor(group(y, g), group(y, g), bank(E_[2], HPG, PS)[0:c], ALU.add).then_inc(v_y1.sem, 1)
                    if running:
                        dve.wait_ge(h_in.sems[g % HPL], h_in.at(g // HPL))
                        hg = hb_[:, g % HPL, :, :].rearrange("p b (h v) -> p b h v", v=PS)
                        el = decay(t, g * HPG, (g + 1) * HPG).unsqueeze(3).to_broadcast([P, NB, HPG, PS])
                    else:
                        hg = h[:, g * HPG:(g + 1) * HPG, :]
                        el = bcast(decay(t, g * HPG, (g + 1) * HPG).rearrange("p a h -> p (a h)"), PS)
                    dve.tensor_tensor(hg, hg, el, ALU.mult).then_inc(v_h0.sem, 1)
                    dve.wait_ge(v_y1.sem, v_y1.at(r, g + 1))
                    dve.wait_ge(v_tmp.sem, v_tmp.at(r, g + 1))
                    dve.tensor_tensor(group(y, g), group(y, g), tmp[0:c, :].rearrange("p (h v) -> p h v", v=PS),
                                              ALU.add).then_inc(v_y2.sem, 1)
                    dve.wait_ge(v_h0.sem, v_h0.at(r, g + 1))
                    for b in range(nseq):
                        dve.wait_ge(m_h.sem, m_h.at(r, nseq * g + b + 1))
                        hv = hb_[:, g % HPL, b, :] if running else h[:, g * HPG:(g + 1) * HPG, :].rearrange("p h v -> p (h v)")
                        dve.tensor_tensor(hv, hv, ps[:, E_[2 - 2 * (b % 2)], :], ALU.add).then_inc(v_h1.sem, 1)
                    dve.wait_ge(m_z.sem, m_z.at(r, g + 1))
                    dve.wait_ge(v_y2.sem, v_y2.at(r, g + 1))
                    dve.tensor_tensor(group(y, g), group(y, g), bank(E_[3], HPG, PS)[0:c], ALU.mult).then_inc(v_yz.sem, 1)

                beta = at("beta", t)
                for g in range(G):
                    dve.wait_ge(m_x.sem, m_x.at(r, g + 1))
                    dve.wait_ge(m_in.sem, m_in.ahead(r))
                    dve.wait_ge(p_wx.sem, p_wx.ahead(r))
                    dve.tensor_tensor(group(xdt, g), bank(E_[g], HPG, PS)[0:c],
                                               bcast(at("dt", t)[:, g * HPG:(g + 1) * HPG], PS), ALU.mult).then_inc(v_xdt.sem, 1)
                if running:
                    dve.wait_ge(loaded.sems[0], 16)
                    for b in range(NB):
                        cols = con["seq_cols"][:, b * TS:(b + 1) * TS]
                        ins = dve.tensor_tensor(cm[:, b, :, :], ch[:, 20:24, :], bmid(cols, G), ALU.mult)
                    ins.then_inc(v_cm.sem, 1)
                    for b in range(NB):
                        cols = con["seq_cols"][:, b * TS:(b + 1) * TS]
                        ins = dve.tensor_tensor(qm[:, b, :, :], ch[:, 24:32, :], bmid(cols, HG), ALU.mult)
                    ins.then_inc(v_qm.sem, 1)
                dve.wait_ge(v_kn.sem, v_kn.at(r))
                dve.wait_ge(m_AV.sem, m_AV.ahead(r))
                dve.wait_ge(m_SU.sem, m_SU.ahead(r))
                dve.tensor_tensor(kbn[0:c, :, :], kn[0:c, :, :], bcast(beta, P), ALU.mult).then_inc(v_kbn.sem, 1)
                for hb in range(2):
                    dve.wait_ge(m_v.sem, m_v.at(r, hb + 1))
                    dve.tensor_tensor(vb[0:c, heads(hb), :], bank(B[hb], NHB, P)[0:c],
                                              bcast(beta[:, heads(hb)], P), ALU.mult).then_inc(v_vb.sem, 1)
                if not first:
                    mean_square(r - 1)
                ssd_weights(0)
                for hb in range(2):
                    dve.wait_ge(a_dec.sem, a_dec.at(r, hb + 1))
                    dve.wait_ge(m_G.sem, m_G.at(r, hb + 1))
                    dve.wait_ge(p_mat.sem, p_mat.ahead(r))
                    dve.tensor_tensor(AT[0:c, heads(hb), :], bank(B[hb], NHB, c)[0:c], dec[0:c, heads(hb), :],
                                              ALU.mult).then_inc(v_AT.sem, 1)
                for hb in range(2):
                    dve.wait_ge(m_QK.sem, m_QK.at(r, hb + 1))
                    dve.tensor_tensor(qkT[0:c, heads(hb), :], bank(A[hb], NHB, c)[0:c], dec[0:c, heads(hb), :],
                                              ALU.mult).then_inc(v_qk.sem, 1)
                if not first:
                    normalise(r - 1)
                for hb in range(2):
                    dve.wait_ge(p_mat.sem, p_mat.at(r, hb + 1))
                    dve.tensor_tensor(TT_[0:c, heads(hb), :], bmid(con["ident"][0:c, 0:c], NHB),
                                              mat[0:c, 0, heads(hb), :], ALU.subtract).then_inc(v_TT.sem, 1)
                if not first:
                    gate_out(r - 1, 1 - u)
                ssd_group(0)
                if running:
                    dve.wait_ge(a_kT.sem, a_kT.at(0))
                    for b in range(NB):
                        cols = con["seq_cols"][:, b * TS:(b + 1) * TS]
                        ins = dve.tensor_tensor(km[:, b, :, :], kT[:, :, :], bmid(cols, HG), ALU.mult)
                    ins.then_inc(v_km.sem, 1)
                ssd_weights(1)
                for l in range(nl):
                    for hb in range(2):
                        if l < nl - 1:
                            dve.wait_ge(m_dT.sem, m_dT.at(r, 2 * l + hb + 1))
                            if l:
                                dve.wait_ge(v_T.sem, v_T.at(r, 2 * l - 1 + hb))
                            else:
                                dve.wait_ge(a_T.sem, a_T.at(r))
                            T_cut = cut(T_[0:c, heads(hb), :], l, False)
                            dve.tensor_tensor(T_cut, T_cut, cut_bank(B[hb], l, False), ALU.subtract).then_inc(v_T.sem, 1)
                        dve.wait_ge(m_dTT.sem, m_dTT.at(r, 2 * l + hb + 1))
                        if l:
                            dve.wait_ge(v_TTn.sem, v_TTn.at(r, 2 * l - 1 + hb))
                        else:
                            dve.wait_ge(v_TT.sem, v_TT.at(r))
                        TT_cut = cut(TT_[0:top(l), heads(hb), :], l, True)
                        dve.tensor_tensor(TT_cut, TT_cut, cut_bank(A[hb], l, True)[0:top(l)], ALU.subtract).then_inc(v_TTn.sem, 1)
                    if l == 4 and not last:
                        kq_sizes(r + 1)
                    if not running and l < 3:
                        ssd_group(l + 1)
                        if l < 2:
                            ssd_weights(l + 2)
                if running:
                    for g in range(1, G):
                        if g > 1:
                            ssd_weights(g)
                        ssd_group(g)
                dve.wait_ge(a_ysq.sem, a_ysq.at(r))
                dve.tensor_scalar(yss[0:c, 1, :], yss[0:c, 0, :], 1.0 / XG, EPS, ALU.mult, ALU.add).then_inc(v_yms.sem, 1)
                for hb in range(2):
                    dve.wait_ge(m_KS.sem, m_KS.at(r, hb + 1))
                    dve.wait_ge(v_vb.sem, v_vb.at(r))
                    dve.wait_ge(v_kss.sem, v_kss.at(r if last else r + 1))
                    for n in range(NHB):
                        hd = NHB * hb + n
                        dve.scalar_tensor_tensor(
                            out=res[0:c, hd, :], in0=bank(B[hb], NHB, P)[0:c, n, :],
                            scalar=tab["nBE"][0:c, bass.ds(t, 1), hd:hd + 1], in1=vb[0:c, hd, :],
                            op0=ALU.mult, op1=ALU.add).then_inc(v_res.sem, 1)
                dve.wait_ge(v_res.sem, v_res.at(r))
                for hb in range(2):
                    dve.wait_ge(m_QS.sem, m_QS.at(r, hb + 1))
                    dve.tensor_tensor(o[0:c, heads(hb), :], bank(B[hb], NHB, P)[0:c],
                                              bcast(at("E", t)[:, HS + NHB * hb:HS + NHB * hb + NHB], P), ALU.mult).then_inc(v_o1.sem, 1)
                if running:
                    dve.wait_ge(state_in.sems[0], state_in.at(0))
                def decay_state(b):
                    dve.tensor_tensor(S[:, b, :, :], S[:, b, :, :], bcast(decay(t, HS, H)[:, b, :], P),
                                      ALU.mult).then_inc(v_S0.sem, 1)

                decay_state(0)
                dve.wait_ge(v_o1.sem, v_o1.at(r))
                for hb in range(2):
                    dve.wait_ge(m_AV.sem, m_AV.at(r, hb + 1))
                    dve.tensor_tensor(o[0:c, heads(hb), :], o[0:c, heads(hb), :], bank(A[hb], NHB, P)[0:c],
                                              ALU.add).then_inc(v_o2.sem, 1)
                for b in range(nseq):
                    if b:
                        decay_state(b)
                    dve.wait_ge(v_S0.sem, v_S0.at(r, b + 1))
                    for hb in range(2):
                        dve.wait_ge(m_SU.sem, m_SU.at(r, 2 * b + hb + 1))
                        dve.tensor_tensor(S[:, b, heads(hb), :], S[:, b, heads(hb), :], bank(B[hb], NHB, P),
                                                  ALU.add).then_inc(v_S1.sem, 1)
                if not last:
                    scale_k(1 - u, r + 1)
                dve.tensor_scalar(rs[0:c, u, 1, :], rs[0:c, u, 1, :], float(P) ** -0.5, None, ALU.mult).then_inc(v_rq.sem, 1)
                dve.wait_ge(v_rq.sem, v_rq.at(r))
                dve.wait_ge(v_o2.sem, v_o2.at(r))
                dve.tensor_tensor(o[0:c, :, :], o[0:c, :, :], bcast(rs[0:c, u, 1, :], P), ALU.mult).then_inc(v_oq.sem, 1)
                for g in range(G):
                    dve.wait_ge(m_yT.sem, m_yT.at(r, g + 1))
                    dve.tensor_tensor(ch[:, XT + GT + 4 * g:XT + GT + 4 * g + 4, :], bank(E_[g], 4, c),
                                              bcast(snw[:, 4 * g:4 * g + 4], c), ALU.mult).then_inc(v_ys.sem, 1)
            kq_sizes(0)
            scale_k(0, 0)
            chunks(dve, body)
            mean_square(last_round)
            normalise(last_round)
            gate_out(last_round, last_place)

        @block.gpsimd
        def _(pool):
            prime(pool, p_y0, p_mat, p_wx, p_kw, p_bm, p_kwm)

            pool.wait_ge(consts_in.sems[0], consts_in.at(0))

            def body(t, u, r, first, last):
                def mask(l):
                    for hb in range(2):
                        hs = slice(NHB * hb, NHB * hb + NHB)
                        if l == 0:
                            pool.wait_ge(v_AT.sem, v_AT.at(r, hb + 1))
                            pool.wait_ge(m_X.sem, m_X.ahead(r))
                        elif l == 1:
                            pool.wait_ge(m_X.sem, m_X.ahead(r))
                        elif l == 2:
                            pool.wait_ge(v_TT.sem, v_TT.at(r, hb + 1))
                        else:
                            pool.wait_ge(m_X.sem, m_X.at(r, 2 * (l - 3) + hb + 1))
                        pool.tensor_tensor(mat[0:c, l % 2, hs, :], AT[0:c, hs, :], bmid(lev[0:c, l, :], NHB),
                                                    ALU.mult).then_inc(p_mat.sem, 1)

                for g in range(G):
                    pool.wait_ge(v_xdt.sem, v_xdt.at(r, g + 1))
                    pool.wait_ge(m_h.sem, m_h.ahead(r))
                    hs = slice(g * HPG, (g + 1) * HPG)
                    pool.tensor_tensor(wx[0:c, hs, :], xdt[0:c, hs, :], bcast(at("W", t)[:, hs], PS), ALU.mult).then_inc(p_wx.sem, 1)
                    pool.wait_ge(a_x.sem, a_x.at(r, g + 1))
                    pool.tensor_tensor(y[0:c, hs, :], y[0:c, hs, :], bcast(drow[0:c, hs], PS), ALU.mult).then_inc(p_y0.sem, 1)
                for l in range(levels):
                    mask(l)
                pool.wait_ge(v_kn.sem, v_kn.at(r))
                pool.wait_ge(m_SU.sem, m_SU.ahead(r))
                pool.tensor_tensor(kw[0:c, :, :], kn[0:c, :, :], bcast(at("W", t)[:, HS:H], P), ALU.mult).then_inc(p_kw.sem, 1)
                if running:
                    pool.wait_ge(a_B.sem, a_B.at(0))
                    for g in range(G):
                        for b in range(NB):
                            if g or b >= 2:
                                pool.wait_ge(m_h.sem, m_h.at(0, NB * g + b - 1))
                            pool.tensor_scalar(bm[0:c, b % 2, :], btok[0:c, g, :], con["seq_rows"][0:c, b:b + 1],
                                                       None, ALU.mult).then_inc(p_bm.sem, 1)
                    pool.wait_ge(p_kw.sem, p_kw.at(0))
                    for n in range(2 * NB):
                        if n >= 2:
                            pool.wait_ge(m_SU.sem, m_SU.at(0, n - 1))
                        hs = slice(NHB * (n % 2), NHB * (n % 2) + NHB)
                        pool.tensor_scalar(kwm[0:c, n % 2, :, :], kw[0:c, hs, :],
                                                    con["seq_rows"][0:c, n // 2:n // 2 + 1], None, ALU.mult).then_inc(p_kwm.sem, 1)

            chunks(pool, body)


class Splitter:

    def __init__(self, nc, sb, tag, source, ku, ahead=2):
        self.source, self.ring = source, ahead
        self.raw = sb(f"{tag}_w", [P, ahead, ku, P])
        self.hi = [sb(f"{tag}_wh{u}", [P, ku, P], F32R) for u in range(2)]
        self.lo = [sb(f"{tag}_wl{u}", [P, ku, P], F32R) for u in range(2)]
        self.loaded = Loads(nc, f"{tag}_w_in", ahead)
        self.hi_done, self.lo_done, self.used = (Event(nc, f"{tag}_{n}") for n in ("w_hi", "w_lo", "w_used"))

    def load(self, sp, s, unit, place):
        if not (isinstance(s, int) and s < self.ring):
            sp.wait_ge(self.lo_done.sem, self.lo_done.ahead(s - self.ring + 1))
        sp.dma_start(self.raw[:, place:place + 1, :, :],
                     self.source[bass.ds(unit, 1)].rearrange("a p k n -> p a k n")).then_inc(self.loaded.sems[place], 16)

    def split_hi(self, act, s, u, place=None, loads=None):
        if place is None:
            place, loads = u, None
        act.wait_ge(self.loaded.sems[place], 8 * (s - u) + 16 if loads is None else 16 * loads)
        if not (isinstance(s, int) and s < 2):
            act.wait_ge(self.used.sem, self.used.ahead(s - 1))
        act.activation(self.hi[u][:, :, :], self.raw[:, place, :, :], ACT.Copy).then_inc(self.hi_done.sem, 1)

    def split_lo(self, dve, s, u, place=None):
        place = u if place is None else place
        dve.wait_ge(self.hi_done.sem, self.hi_done.at(s))
        if not (isinstance(s, int) and s < 2):
            dve.wait_ge(self.used.sem, self.used.ahead(s - 1))
        dve.tensor_tensor(self.lo[u][:, :, :], self.raw[:, place, :, :], self.hi[u][:, :, :].bitcast(F32),
                                          ALU.subtract).then_inc(self.lo_done.sem, 1)

    def product(self, pe, u, out, hi, lo, first=True, last=True):
        ku = self.raw.shape[2]
        for k in range(ku):
            for a, (l, r) in enumerate(((self.hi[u], hi), (self.hi[u], lo), (self.lo[u], hi))):
                ins = pe.matmul(out, l[:, k, :], r(k), start=(first and k == 0 and a == 0),
                                stop=(last and k == ku - 1 and a == 2))
        return ins


def deep_phase(nc, tag, source, ku, nu, w_in, groups, gates=None, hi=None, lo=None, x=None):
    CN = NCOL[0][1]
    ng, total, pairs = max(groups) + 1, 3 * KD * nu, KD // 2
    with phase(nc) as ctx:
        sb = allocator(ctx, nc)
        raw = sb(f"{tag}_raw", [P, nu, ku, CN])
        yh, yl = sb(f"{tag}_yh", [P, ku * nu, CN], F32R), sb(f"{tag}_yl", [P, ku * nu, CN], F32R)
        ahead = nu if nu > 2 else 2 * nu
        ring = Splitter(nc, sb, tag, w_in, ku, ahead)
        if gates is not None:
            sg, v = (sb(f"{tag}_{n}", [P, 2, m, CN]) for n, m in (("sg", 2), ("v", 1)))
        ps = ctx.enter_context(nc.psum_tensor(f"{tag}_ps", [P, 2 * ng, 512], F32))
        raw_in, sg_in = Loads(nc, f"{tag}_raw_in", nu), Loads(nc, f"{tag}_sg_in", 2)
        y_hi, y_lo = Event(nc, f"{tag}_y_hi"), Event(nc, f"{tag}_y_lo")

        def pair(name, per=1):
            return [Event(nc, f"{tag}_{name}{u}", per) for u in range(2)]

        read, summed, hi_done, lo_done = pair("read", ng), pair("summed"), pair("hi_done"), pair("lo_done")
        block = ctx.enter_context(nc.Block())

        def steps(eng, start, body):
            for n in range(3):
                start(n)
                with eng.Fori(0, pairs - 1) as i:
                    for u in range(2):
                        body(n, 2 * i + u, u, pairs * n + i, (KD * n + 2 * i + u) * nu)
                for u in range(2):
                    body(n, KD - 2 + u, u, pairs * (n + 1) - 1, (KD * (n + 1) - 2 + u) * nu)

        def place(u, unit):
            return (u * nu + unit) % 2

        def raw_place(u, unit):
            return unit if ahead == nu else u * nu + unit

        def after_next(n, m, u, rnd, s0, unit):
            on, unit_ = divmod(unit + 2, nu)
            tile, rnd_, u_ = (KD * n + m + 1, rnd + u, 1 - u) if on else (KD * n + m, rnd, u)
            return s0 + unit + 2, place(u_, unit_), raw_place(u_, unit_), (tile if ahead == nu else rnd_) + 1

        @block.sync
        def _(sp):
            for s in range(ahead):
                if s == 2:
                    sp.wait_ge(raw_in.sems[0], raw_in.at(0))
                ring.load(sp, s, s, s)

            def body(n, m, u, rnd, s0):
                if gates is not None:
                    c0, cn = NCOL[n]
                    sp.wait_ge(summed[u].sem, summed[u].ahead(rnd))
                    for a in range(2):
                        sp.dma_start(sg[:, u, a:a + 1, 0:cn], gates[bass.ds(m + KD * a, 1), :, c0:c0 + cn]
                                              .rearrange("g p n -> p g n")).then_inc(sg_in.sems[u], 16)
                for unit in range(nu):
                    s = s0 + unit
                    if isinstance(s, int) and s + ahead >= total:
                        continue
                    at = (s + ahead) % (KD * nu) if isinstance(s, int) else s + ahead - n * KD * nu
                    ring.load(sp, s + ahead, at, raw_place(u, unit))

            steps(sp, lambda n: None, body)

        @block.gpsimd
        def _(pool):
            for n, (c0, cn) in enumerate(NCOL):
                for y in range(nu):
                    if n:
                        pool.wait_ge(y_lo.sem, y_lo.at(nu * (n - 1) + y))
                    pool.dma_start(raw[:, y, :, 0:cn], source[y * ku:(y + 1) * ku, :, c0:c0 + cn].rearrange(
                        "k p n -> p k n")).then_inc(raw_in.sems[y], 16)

        @block.tensor
        def _(pe):
            prime(pe, ring.used)

            def body(n, m, u, rnd, s0):
                cn = NCOL[n][1]
                pe.wait_ge(read[u].sem, read[u].ahead(rnd))
                for unit in range(nu):
                    g = groups[unit]
                    pe.wait_ge(ring.lo_done.sem, ring.lo_done.at(s0 + unit))
                    pe.wait_ge(y_lo.sem, y_lo.at(nu * n + unit))
                    ins = ring.product(pe, place(u, unit), ps[:, ng * u + g, 0:cn],
                                       lambda k: yh[:, unit * ku + k, 0:cn], lambda k: yl[:, unit * ku + k, 0:cn],
                                       unit == 0 or groups[unit - 1] != g, unit == nu - 1 or groups[unit + 1] != g)
                    ins.then_inc(ring.used.sem, 1)

            steps(pe, lambda n: None, body)

        def end_of(s0):
            return s0 + nu - 1

        @block.scalar
        def _(act):
            prime(act, y_hi, *hi_done, ring.hi_done)
            for s in range(2):
                ring.split_hi(act, s, s, s, 1)

            def convert(n, unit):
                cn, k = NCOL[n][1], unit * ku
                act.wait_ge(raw_in.sems[unit], raw_in.at(n))
                if n:
                    act.wait_ge(ring.used.sem, ring.used.at((KD * n - 1) * nu + unit))
                act.activation(yh[:, k:k + ku, 0:cn], raw[:, unit, :, 0:cn], ACT.Copy).then_inc(y_hi.sem, 1)

            def start(n):
                for unit in range(nu if n == 0 else 0):
                    convert(n, unit)

            def body(n, m, u, rnd, s0):
                c0, cn = NCOL[n]
                for unit in range(nu):
                    s, parts, at, loads = after_next(n, m, u, rnd, s0, unit)
                    if not (isinstance(s, int) and s >= total):
                        ring.split_hi(act, s, parts, at, loads)
                    if isinstance(m, int) and m == KD - 1 and n < 2:
                        convert(n + 1, unit)
                if gates is not None:
                    act.wait_ge(summed[u].sem, summed[u].at(rnd))
                    act.activation(hi[:, bass.ds(m, 1), c0:c0 + cn], v[:, u, :, 0:cn], ACT.Copy).then_inc(hi_done[u].sem, 1)

            steps(act, start, body)

        @block.vector
        def _(dve):
            prime(dve, y_lo, *read, *summed, *lo_done, ring.lo_done)
            for s in range(2):
                ring.split_lo(dve, s, s, s)

            def convert(n, unit):
                cn, k = NCOL[n][1], unit * ku
                dve.wait_ge(y_hi.sem, y_hi.at(nu * n + unit))
                dve.tensor_tensor(yl[:, k:k + ku, 0:cn], raw[:, unit, :, 0:cn],
                                  yh[:, k:k + ku, 0:cn].bitcast(F32), ALU.subtract).then_inc(y_lo.sem, 1)

            def start(n):
                for unit in range(nu if n == 0 else 0):
                    convert(n, unit)

            def body(n, m, u, rnd, s0):
                c0, cn = NCOL[n]
                for unit in range(nu):
                    s, parts, at, _ = after_next(n, m, u, rnd, s0, unit)
                    if not (isinstance(s, int) and s >= total):
                        ring.split_lo(dve, s, parts, at)
                    if isinstance(m, int) and m == KD - 1 and n < 2:
                        convert(n + 1, unit)
                dve.wait_ge(ring.used.sem, ring.used.at(end_of(s0)))
                if gates is None:
                    xv = x[:, bass.ds(m, 1), c0:c0 + cn]
                    dve.tensor_tensor(xv, xv, ps[:, u:u + 1, 0:cn], ALU.add).then_inc(read[u].sem, 1)
                    return
                dve.wait_ge(sg_in.sems[u], 32 * rnd + 32)
                for a in range(2):
                    dve.tensor_tensor(sg[:, u, a, 0:cn], ps[:, 2 * u + a, 0:cn], sg[:, u, a, 0:cn], ALU.mult).then_inc(read[u].sem, 1)
                dve.wait_ge(read[u].sem, read[u].at(rnd))
                dve.wait_ge(lo_done[u].sem, lo_done[u].ahead(rnd))
                dve.tensor_tensor(v[:, u, 0, 0:cn], sg[:, u, 0, 0:cn], sg[:, u, 1, 0:cn], ALU.add).then_inc(summed[u].sem, 1)
                dve.wait_ge(hi_done[u].sem, hi_done[u].at(rnd))
                dve.tensor_tensor(lo[:, bass.ds(m, 1), c0:c0 + cn], v[:, u, :, 0:cn],
                                                hi[:, bass.ds(m, 1), c0:c0 + cn].bitcast(F32), ALU.subtract).then_inc(lo_done[u].sem, 1)

            steps(dve, start, body)


def residual_phase(nc, d, hi, lo, x):
    with phase(nc) as ctx:
        sb = allocator(ctx, nc)
        ring = Splitter(nc, sb, "wo", d["w_o"], KD)
        ps = ctx.enter_context(nc.psum_tensor("wo_ps", [P, 6, 512], F32))
        x_in = Loads(nc, "wo_x_in", 1)
        product, added = Event(nc, "wo_product", 3), Event(nc, "wo_added", 3)
        block = ctx.enter_context(nc.Block())

        @block.sync
        def _(sp):
            for m in range(2):
                ring.load(sp, m, m, m)
            sp.dma_start(x[:, :, :], d["x"]).then_inc(x_in.sems[0], 16)
            with sp.Fori(0, KD // 2 - 1) as i:
                for u in range(2):
                    ring.load(sp, 2 * i + u + 2, 2 * i + u + 2, u)

        def tiles(eng, body):
            with eng.Fori(0, KD // 2 - 1) as i:
                for u in range(2):
                    body(2 * i + u, u, i)
            for u in range(2):
                body(KD - 2 + u, u, KD // 2 - 1)

        @block.tensor
        def _(pe):
            prime(pe, product, ring.used)

            def body(m, u, i):
                pe.wait_ge(ring.lo_done.sem, ring.lo_done.at(m))
                for n, (c0, cn) in enumerate(NCOL):
                    if not (isinstance(m, int) and m < 2):
                        pe.wait_ge(added.sem, added.ahead(2 * i))
                    ins = ring.product(pe, u, ps[:, 3 * u + n, 0:cn], lambda k: hi[:, k, c0:c0 + cn],
                                       lambda k: lo[:, k, c0:c0 + cn])
                    if n < 2:
                        ins.then_inc(product.sem, 1)
                ins.then_inc(ring.used.sem, 1)

            tiles(pe, body)

        @block.scalar
        def _(act):
            prime(act, ring.hi_done)
            ring.split_hi(act, 0, 0)

            def body(m, u, i):
                if not (isinstance(m, int) and m == KD - 1):
                    ring.split_hi(act, m + 1, 1 - u)

            tiles(act, body)

        @block.vector
        def _(dve):
            prime(dve, added, ring.lo_done)
            ring.split_lo(dve, 0, 0)
            dve.wait_ge(x_in.sems[0], x_in.at(0))

            def body(m, u, i):
                if not (isinstance(m, int) and m == KD - 1):
                    ring.split_lo(dve, m + 1, 1 - u)
                dve.wait_ge(ring.used.sem, ring.used.at(m))
                for n, (c0, cn) in enumerate(NCOL):
                    xv = x[:, bass.ds(m, 1), c0:c0 + cn]
                    dve.tensor_tensor(xv, xv, ps[:, 3 * u + n:3 * u + n + 1, 0:cn], ALU.add).then_inc(added.sem, 1)

            tiles(dve, body)


def up_phase(nc, d, hi, lo, ffn):
    UW, UP = 2 + TP + 6 * NB, TP + 6 * NB
    with phase(nc) as ctx:
        sb = allocator(ctx, nc)
        ring = Splitter(nc, sb, "up", d["w_up"], KD)
        U, Y, gt, f = sb("uU", [P, UW]), sb("uY", [P, 2, UW]), sb("ug", [P, T]), sb("uf", [P, T])
        old, new = sb("uold", [P, FT, NB * 2]), sb("unew", [P, FT, 18])
        cw, cb, spare = sb("ucw", [P, FT, W3]), sb("ucb", [P, FT]), sb("uspare", [P, 2])
        ps = ctx.enter_context(nc.psum_tensor("u_ps", [P, 6, 512], F32))
        consts_in, stored, new_out = Loads(nc, "u_consts_in", 1, 3), Loads(nc, "u_stored", 1, primed=16), Loads(nc, "u_new_out", 1)
        zero, evacuated, old_put, new_got, tap, silu, gated = (Event(nc, f"u_{n}", k) for n, k in (
            ("zero", 1), ("evacuated", 4), ("old_put", 1), ("new_got", 2), ("tap", W3), ("silu", 2), ("gated", 3)))
        block = ctx.enter_context(nc.Block())

        def seqs(ap):
            return ap[:, UW - 6 * NB:UW].rearrange("p (b t) -> p b t", t=6)

        def rounds(eng, body):
            with eng.Fori(0, FT - 1) as j:
                body(j)
            body(FT - 1)

        @block.sync
        def _(sp):
            stored.prime(sp)
            for m in range(2):
                ring.load(sp, m, m, m)
            sp.dma_start(cw[:, :, :], d["ffn_w"]).then_inc(consts_in.sems[0], 16)
            sp.dma_start(cb[:, :], d["ffn_b"]).then_inc(consts_in.sems[0], 16)
            sp.dma_start(old[:, :, :], d["ffn_old"]).then_inc(consts_in.sems[0], 16)

            def body(j):
                if not isinstance(j, int):
                    for u in range(2):
                        ring.load(sp, 2 * j + u + 2, 2 * j + u + 2, u)
                sp.wait_ge(gated.sem, gated.at(j))
                sp.dma_start(ffn[bass.ds(j, 1)].rearrange("a p n -> p (a n)"), f[:, :]).then_inc(stored.sems[0], 16)

            rounds(sp, body)
            sp.wait_ge(new_got.sem, new_got.at(FT - 1))
            sp.dma_start(d["ffn_new"], new[:, :, :]).then_inc(new_out.sems[0], 16)
            sp.wait_ge(stored.sems[0], stored.at(FT - 1))
            sp.wait_ge(new_out.sems[0], new_out.at(0))

        @block.tensor
        def _(pe):
            prime(pe, ring.used)

            def body(j):
                for u in range(2):
                    pe.wait_ge(ring.lo_done.sem, ring.lo_done.at(2 * j + u))
                    reader = (evacuated, gated)[u]
                    pe.wait_ge(reader.sem, reader.ahead(j))
                    for n, (c0, cn) in enumerate(NCOL):
                        ins = ring.product(pe, u, ps[:, 3 * u + n, 0:cn], lambda k: hi[:, k, c0:c0 + cn],
                                           lambda k: lo[:, k, c0:c0 + cn])
                    ins.then_inc(ring.used.sem, 1)

            rounds(pe, body)

        @block.scalar
        def _(act):
            prime(act, evacuated, silu, ring.hi_done)
            act.wait_ge(zero.sem, zero.at(0))
            act.activation(spare[:, 1:2], spare[:, 0:1], ACT.Silu)
            ring.split_hi(act, 0, 0)

            def body(j):
                ring.split_hi(act, 2 * j + 1, 1)
                act.wait_ge(ring.used.sem, ring.used.at(2 * j))
                act.wait_ge(tap.sem, tap.ahead(j))
                act.wait_ge(new_got.sem, new_got.ahead(j))
                for n, (c0, cn) in enumerate(NCOL):
                    cp = min(cn, TP - c0)
                    act.activation(U[:, 2 + c0:2 + c0 + cp], ps[:, n, 0:cp], ACT.Copy).then_inc(evacuated.sem, 1)
                act.activation(seqs(U)[:, :, 2:6], ps[:, 2, TP - 716:TP - 716 + TS].rearrange(
                    "p (b t) -> p b t", t=NT), ACT.Copy).then_inc(evacuated.sem, 1)
                if not isinstance(j, int):
                    ring.split_hi(act, 2 * j + 2, 0)
                act.wait_ge(tap.sem, tap.at(j))
                act.wait_ge(gated.sem, gated.ahead(j))
                act.activation(gt[:, 0:TP], Y[:, 0, 0:TP], ACT.Silu).then_inc(silu.sem, 1)
                act.activation(gt[:, TP:T].rearrange("p (b t) -> p b t", t=NT),
                                       seqs(Y[:, 0, :])[:, :, 0:NT], ACT.Silu).then_inc(silu.sem, 1)

            rounds(act, body)

        @block.vector
        def _(dve):
            prime(dve, zero, tap, gated, ring.lo_done)
            dve.memset(U[:, 0:2], 0.0)
            dve.memset(spare[:, :], 0.0).then_inc(zero.sem, 1)
            ring.split_lo(dve, 0, 0)
            dve.wait_ge(consts_in.sems[0], consts_in.at(0))
            dve.wait_ge(zero.sem, zero.at(0))

            def body(j):
                ring.split_lo(dve, 2 * j + 1, 1)
                dve.wait_ge(evacuated.sem, evacuated.at(j))
                dve.wait_ge(old_put.sem, old_put.at(j))
                dve.wait_ge(silu.sem, silu.ahead(j))
                dve.tensor_scalar(Y[:, 0, 0:UP], U[:, 0:UP], cw[:, bass.ds(j, 1), 0:1], cb[:, bass.ds(j, 1)],
                                         ALU.mult, ALU.add).then_inc(tap.sem, 1)
                for n in range(1, W3):
                    dve.wait_ge(tap.sem, tap.at(j, n))
                    dve.scalar_tensor_tensor(out=Y[:, n % 2, 0:UP], in0=U[:, n:n + UP],
                                                    scalar=cw[:, bass.ds(j, 1), n:n + 1], in1=Y[:, 1 - n % 2, 0:UP],
                                                    op0=ALU.mult, op1=ALU.add).then_inc(tap.sem, 1)
                if not isinstance(j, int):
                    ring.split_lo(dve, 2 * j + 2, 0)
                dve.wait_ge(silu.sem, silu.at(j))
                dve.wait_ge(ring.used.sem, ring.used.at(2 * j + 1))
                dve.wait_ge(stored.sems[0], stored.ahead(j))
                for n, (c0, cn) in enumerate(NCOL):
                    dve.tensor_tensor(f[:, c0:c0 + cn], gt[:, c0:c0 + cn], ps[:, 3 + n, 0:cn], ALU.mult).then_inc(gated.sem, 1)

            rounds(dve, body)

        @block.gpsimd
        def _(pool):
            prime(pool, old_put, new_got)
            pool.wait_ge(consts_in.sems[0], consts_in.at(0))
            with pool.Fori(0, FT) as j:
                pool.wait_ge(tap.sem, tap.ahead(j))
                pool.tensor_copy(seqs(U)[:, :, 0:2],
                                            old[:, bass.ds(j, 1), :].rearrange("p a (b t) -> p (a b) t", t=2)).then_inc(old_put.sem, 1)
                pool.wait_ge(evacuated.sem, evacuated.at(j))
                pool.tensor_copy(new[:, bass.ds(j, 1), 0:2], U[:, TP:TP + 2].unsqueeze(1)).then_inc(new_got.sem, 1)
                pool.tensor_copy(new[:, bass.ds(j, 1), 2:18].rearrange("p a (b t) -> p (a b) t", t=2),
                                            seqs(U)[:, :, 4:6]).then_inc(new_got.sem, 1)


def tail_phases(nc, d, ones, scratch, mixed):
    ffn = nc.dram_tensor("ffn", [FT, P, T], F32, kind="Internal").ap()
    with ExitStack() as whole:
        with ExitStack() as to_residual:
            hi, lo = (to_residual.enter_context(nc.sbuf_tensor(n, [P, KD, T], F32R, side="right")) for n in ("m_hi", "m_lo"))
            deep_phase(nc, "merge", mixed, KD, 3, d["w_out"], (0, 0, 1), gates=scratch[NSCAN:], hi=hi, lo=lo)
            x = allocator(whole, nc)("x2", [P, KD, T])
            residual_phase(nc, d, hi, lo, x)
        with ExitStack() as to_up:
            sb = allocator(to_up, nc)
            hi, lo = sb("f_hi", [P, KD, T], F32R), sb("f_lo", [P, KD, T], F32R)
            norm_phase(nc, "ffnnorm", x, d["norm_ffn"], ones, hi, lo)
            up_phase(nc, d, hi, lo, ffn)
        deep_phase(nc, "down", ffn, FT // 2, 2, d["w_down"], (0, 0), x=x)
        norm_phase(nc, "lastnorm", x, d["norm_f"], ones, out=d["y"])


MASKS = (("ident", P, F32), ("tri", C, F32), ("tri_s", TS, F32), ("same", TS, F32), ("seq_wide", NB * P, F32),
         ("identb", P, BF16), ("late", C, BF16), ("late_s", TS, BF16), ("levels", 7 * C, BF16),
         ("levels_s", 2 * TS, BF16), ("seq_cols", NB * TS, F32), ("seq_rows", NB, F32))
N_MASK = sum(n for _, n, _ in MASKS)
GATES_ONLY = ("tri", "tri_s", "same", "seq_wide")


def masks_of_shapes():
    i, j = np.arange(P)[:, None], np.arange(P)[None, :]
    seq = i // NT == j // NT
    level = [(i // (2 * s) == j // (2 * s)) & (i % (2 * s) < s) & (j % (2 * s) >= s) for s in (1, 2, 4, 8, 16, 32, 64)]
    owner = np.arange(TS)[None, :] // NT
    m = {
        "ident": i == j, "tri": (i <= j)[:, :C], "tri_s": ((i <= j) & seq)[:, :TS], "same": seq[:, :TS],
        "seq_wide": np.repeat(i // NT == np.arange(NB)[None, :], P, axis=1), "identb": i == j,
        "late": ((j < i) * -1e30)[:, :C], "late_s": ((~seq | (j < i)) * -1e30)[:, :TS],
        "levels": np.concatenate([x[:, :C] for x in level], 1),
        "levels_s": np.concatenate([x[:, :TS] for x in level[:2]], 1),
        "seq_cols": np.concatenate([np.repeat(owner == b, P, axis=0) for b in range(NB)], 1),
        "seq_rows": i // NT == np.arange(NB)[None, :],
    }
    return np.concatenate([np.asarray(m[n], np.float32) for n, _, _ in MASKS], 1)


def ones_phase(nc, ones):
    with phase(nc) as ctx:
        block = ctx.enter_context(nc.Block())

        @block.vector
        def _(dve):
            dve.memset(ones[:, :], 1.0)


def program(nc, d):
    scratch = nc.dram_tensor("projected", [NTILE, P, T], F32, kind="Internal").ap()
    mixed = nc.dram_tensor("mixed", [ZT + OT, P, T], F32, kind="Internal").ap()
    with ExitStack() as whole:
        sb = allocator(whole, nc)
        con = {n: sb(f"c_{n}", [P, c], dt) for n, c, dt in MASKS if n not in GATES_ONLY}
        con["ones"], con["selT"] = sb("c_ones", [P, P]), sb("c_selT", [P, H, C], BF16)
        with ExitStack() as to_scan:
            sb = allocator(to_scan, nc)
            tab = {"E": sb("t_E", [P, NC + 1, H]), "W": sb("t_W", [P, NC + 1, H]), "EL": sb("t_EL", [P, NC + NB, H]),
                   "dt": sb("t_dt", [P, NC + 1, HS]), "beta": sb("t_beta", [P, NC + 1, HG]),
                   "nBE": sb("t_nBE", [P, NC + 1, HG]),
                   "accT": sb("t_accT", [P, T], BF16), "naccT": sb("t_naccT", [P, T], BF16)}
            with ExitStack() as to_project:
                sb = allocator(to_project, nc)
                hi, lo = sb("h_hi", [P, KD, T], F32R), sb("h_lo", [P, KD, T], F32R)
                with ExitStack() as to_gates:
                    sbg = allocator(to_gates, nc)
                    con.update({n: sbg(f"c_{n}", [P, c], dt) for n, c, dt in MASKS if n in GATES_ONLY})
                    with ExitStack() as for_norm:
                        x = allocator(for_norm, nc)("x_T", [P, KD, T])
                        norm_phase(nc, "mixnorm", x, d["norm_mix"], con["ones"], hi, lo, x_in=d["x"],
                                   con=con, masks=d["masks"])
                    gates_phase(nc, d, hi, lo, tab, dict(con, seq_wide=con["seq_wide"][:, :].rearrange(
                        "p (b q) -> p b q", b=NB)))
                project_phase(nc, d, hi, lo, scratch)
            scan_phase(nc, d, tab, con, scratch, mixed, False)
            scan_phase(nc, d, tab, con, scratch, mixed, True)
    with ExitStack() as tail:
        ones = allocator(tail, nc)("tail_ones", [P, P])
        ones_phase(nc, ones)
        tail_phases(nc, d, ones, scratch, mixed)


def kernel(x_prompt, x_sample, state_ssm, state_ssm_conv, state_gdn, state_gdn_conv, state_ffn_conv, meta_tokens,
           norm_mix_w, w_in, ssm_conv_w, ssm_conv_b, ssm_dt_bias, ssm_a_log, ssm_d, ssm_norm_w, gdn_conv_w,
           gdn_dt_bias, gdn_a_log, gdn_norm_w, w_ssm_out, w_gdn_out, w_o, norm_ffn_w, w_up, ffn_conv_w,
           ffn_conv_b, w_down, norm_f_w):
    import concourse.bacc as bacc
    from concourse.bass_utils import run_bass_kernel_spmd

    f32 = np.float32

    def arr(x):
        return np.asarray(x)

    def channel_tiles(x, lead=0):
        x = np.moveaxis(arr(x), -1, 0)
        return np.ascontiguousarray(np.moveaxis(x.reshape((-1, P) + x.shape[1:]), 0, 1))

    def weight_tiles(w):
        k, m = w.shape[0] // P, w.shape[1] // P
        return np.ascontiguousarray(w.reshape(k, P, m, P).transpose(2, 1, 0, 3))

    def units(w, ku):
        w = weight_tiles(w)
        m, _, k, _ = w.shape
        return np.ascontiguousarray(w.reshape(m, P, k // ku, ku, P).transpose(0, 2, 1, 3, 4)).reshape(-1, P, ku, P)

    wi = arr(w_in)[0]
    at = np.cumsum([0, DI, XT * P, HS, GT * P, HG, HG, HG * P, DM, DM])
    z, xbc, dt, qkv, a, b, gate, mg_s, mg_g = (wi[:, at[n]:at[n + 1]] for n in range(9))
    small = np.concatenate([dt, a, b], 1)
    d = {
        "x": channel_tiles(np.concatenate([arr(meta_tokens), arr(x_prompt)[0], arr(x_sample).reshape(TS, DM)], 0)),
        "masks": masks_of_shapes(),
        "norm_mix": channel_tiles(arr(norm_mix_w)[0]),
        "norm_ffn": channel_tiles(arr(norm_ffn_w)[0]),
        "norm_f": channel_tiles(arr(norm_f_w)),
        "w_small": np.ascontiguousarray(small.reshape(KD, P, 48).transpose(1, 0, 2)),
        "gate_bias": np.concatenate([arr(ssm_dt_bias)[0], arr(gdn_dt_bias)[0], np.zeros(HG, f32)])[None],
        "a_log": np.concatenate([arr(ssm_a_log)[0], arr(gdn_a_log)[0]])[None],
        "w_in": weight_tiles(np.concatenate([xbc, qkv, z, gate, mg_s, mg_g], 1)),
        "conv_w": channel_tiles(np.concatenate([arr(ssm_conv_w)[0], arr(gdn_conv_w)[0]], 1)),
        "conv_b": channel_tiles(np.concatenate([arr(ssm_conv_b)[0], np.zeros(GT * P, f32)])),
        "conv_old": channel_tiles(np.concatenate([arr(state_ssm_conv)[0], arr(state_gdn_conv)[0]], 2)).reshape(
            P, XT + GT, NB * 3),
        "ssm_d": arr(ssm_d),
        "ssm_norm": channel_tiles(arr(ssm_norm_w)[0]),
        "gdn_norm": np.ascontiguousarray(arr(gdn_norm_w).T),
        "ssm_old": np.ascontiguousarray(arr(state_ssm)[0].transpose(0, 3, 1, 2)).reshape(NB, P, DI),
        "gdn_old": np.ascontiguousarray(arr(state_gdn)[0].transpose(0, 2, 1, 3)).reshape(NB, P, HG * P),
        "w_out": units(np.concatenate([arr(w_ssm_out)[0], arr(w_gdn_out)[0]], 0), KD),
        "w_o": weight_tiles(arr(w_o)[0]),
        "w_up": weight_tiles(arr(w_up)[0])[np.arange(2 * FT).reshape(2, FT).T.ravel()],
        "ffn_w": channel_tiles(arr(ffn_conv_w)[0]),
        "ffn_b": channel_tiles(arr(ffn_conv_b)[0]),
        "ffn_old": channel_tiles(arr(state_ffn_conv)[0]).reshape(P, FT, NB * 2),
        "w_down": units(arr(w_down)[0], FT // 2),
    }
    outs = {"y": (P, KD, T), "conv_new": (P, XT + GT, 27), "ssm_new": (NB + 1, P, DI), "gdn_new": (NB + 1, P, HG * P),
            "ffn_new": (P, FT, 18)}
    nc = bacc.Bacc("TRN2", target_bir_lowering=False, num_devices=1)
    aps = {n: nc.dram_tensor(f"in_{n}", v.shape, F32, kind="ExternalInput").ap() for n, v in d.items()}
    aps |= {n: nc.dram_tensor(f"out_{n}", s, F32, kind="ExternalOutput").ap() for n, s in outs.items()}
    program(nc, aps)
    got = run_bass_kernel_spmd(nc, [{f"in_{n}": v for n, v in d.items()}], core_ids=[0]).results[0]
    y, conv, ssm, gdn, ffn = (np.asarray(got[f"out_{n}"]) for n in outs)

    def rows(x, first, n):
        return x[:, first:first + n].transpose(2, 1, 0).reshape(x.shape[2], n * P)

    y = y.transpose(2, 1, 0).reshape(T, DM)
    ssm = ssm.reshape(NB + 1, P, HS, PS).transpose(0, 2, 3, 1)
    gdn = gdn.reshape(NB + 1, P, HG, P).transpose(0, 2, 1, 3)
    xbc_n, qkv_n, ffn_n = rows(conv, 0, XT), rows(conv, XT, GT), rows(ffn, 0, FT)
    prompt = (ssm[None, :1], xbc_n[None, None, :3], gdn[None, :1], qkv_n[None, None, :3], ffn_n[None, None, :2])
    running = (ssm[None, 1:], xbc_n[3:].reshape(1, NB, 3, XT * P), gdn[None, 1:],
               qkv_n[3:].reshape(1, NB, 3, GT * P), ffn_n[2:].reshape(1, NB, 2, FF))
    return tuple(np.ascontiguousarray(v) for v in (
        y[None, META:TP], y[TP:].reshape(NB, NT, DM), *prompt, *running))
```
